# Optimizing a Trainium2 kernel written in Bass

```python
import math
import jax, jax.numpy as jnp
from jax import lax
import numpy as np

D_MODEL = 1024
BATCH = 1
SEQ = 256
DEPTH = 2

N_A_LAYERS = DEPTH // 2
N_B_LAYERS = DEPTH - N_A_LAYERS
HEAD_DIM = 64
DIFF_HEADS = D_MODEL // (2 * HEAD_DIM)
MOBA_HEADS = D_MODEL // HEAD_DIM
D_FF = 2816
ROPE_THETA = 10000.0
MOBA_BLOCK = 256
MOBA_TOPK = 3
DIFF_Q_CHUNK = 128
MOBA_Q_CHUNK = 64
FFN_RESIDUAL_SCALE = 0.5
NORM_EPS = 1e-6

kernel_name = "yoco_diffattn_moba_macaron_sandwich"

def rms_norm(x, g):
    xf = x.astype(jnp.float32)
    y = xf * lax.rsqrt(jnp.mean(xf * xf, axis=-1, keepdims=True) + NORM_EPS)
    return (y * g.astype(jnp.float32)).astype(x.dtype)

def rope_tables(seq, dim):
    pos = jnp.arange(seq, dtype=jnp.float32)
    inv_freq = 1.0 / (ROPE_THETA ** (jnp.arange(0, dim, 2, dtype=jnp.float32) / dim))
    ang = pos[:, None] * inv_freq[None, :]
    ang = jnp.concatenate([ang, ang], axis=-1)
    return jnp.cos(ang), jnp.sin(ang)

def apply_rope(x, cos, sin):
    c = cos[None, :, None, :].astype(x.dtype)
    s = sin[None, :, None, :].astype(x.dtype)
    x1, x2 = jnp.split(x, 2, axis=-1)
    rot = jnp.concatenate([-x2, x1], axis=-1)
    return x * c + rot * s

def macaron_half_ffn(x, g_pre, g_post, w_in, w_out):
    h = rms_norm(x, g_pre)
    gu = h @ w_in
    gate, up = jnp.split(gu, 2, axis=-1)
    y = (jax.nn.silu(gate) * up) @ w_out
    return x + FFN_RESIDUAL_SCALE * rms_norm(y, g_post)

def diff_attention(h, w_qkv, lam_vecs, subln, w_o, lam_init, cos, sin):
    B, S, _ = h.shape
    H, Dh = DIFF_HEADS, HEAD_DIM
    q, k, v = jnp.split(h @ w_qkv, 3, axis=-1)
    q = apply_rope(q.reshape(B, S, 2 * H, Dh), cos, sin).transpose(0, 2, 1, 3)
    k = apply_rope(k.reshape(B, S, 2 * H, Dh), cos, sin).transpose(0, 2, 1, 3)
    v = v.reshape(B, S, H, 2 * Dh).transpose(0, 2, 1, 3)
    lv = lam_vecs.astype(jnp.float32)
    lam = jnp.exp(jnp.sum(lv[0] * lv[1])) - jnp.exp(jnp.sum(lv[2] * lv[3])) + lam_init
    nq = S // DIFF_Q_CHUNK
    q_chunks = q.reshape(B, 2 * H, nq, DIFF_Q_CHUNK, Dh).transpose(2, 0, 1, 3, 4)
    kpos = jnp.arange(S)
    scale = Dh ** -0.5

    def one_chunk(args):
        c, qc = args
        qpos = c * DIFF_Q_CHUNK + jnp.arange(DIFF_Q_CHUNK)
        s = jnp.einsum('bhqd,bhkd->bhqk', qc, k).astype(jnp.float32) * scale
        s = jnp.where(kpos[None, :] <= qpos[:, None], s, -jnp.inf)
        p = jax.nn.softmax(s, axis=-1).reshape(B, H, 2, DIFF_Q_CHUNK, S)
        a = p[:, :, 0] - lam * p[:, :, 1]
        return jnp.einsum('bhqk,bhkd->bhqd', a.astype(v.dtype), v)

    o = lax.map(one_chunk, (jnp.arange(nq), q_chunks))
    o = o.transpose(1, 0, 3, 2, 4).reshape(B, S, H, 2 * Dh)
    o = rms_norm(o, subln) * (1.0 - lam_init)
    return o.reshape(B, S, D_MODEL) @ w_o

def shared_kv(x, kv_norm, kv_w, cos, sin):
    B, S, _ = x.shape
    H, Dh = MOBA_HEADS, HEAD_DIM
    k, v = jnp.split(rms_norm(x, kv_norm) @ kv_w, 2, axis=-1)
    k = apply_rope(k.reshape(B, S, H, Dh), cos, sin).transpose(0, 2, 1, 3)
    v = v.reshape(B, S, H, Dh).transpose(0, 2, 1, 3)
    nb = -(-S // MOBA_BLOCK)
    pad = nb * MOBA_BLOCK - S
    k = jnp.pad(k, ((0, 0), (0, 0), (0, pad), (0, 0)))
    v = jnp.pad(v, ((0, 0), (0, 0), (0, pad), (0, 0)))
    kb = k.reshape(B, H, nb, MOBA_BLOCK, Dh)
    vb = v.reshape(B, H, nb, MOBA_BLOCK, Dh)
    kmean = jnp.mean(kb.astype(jnp.float32), axis=3).astype(kb.dtype)
    return kb, vb, kmean

def moba_attention(h, w_q, w_o, kb, vb, kmean, cos, sin):
    B, S, _ = h.shape
    H, Dh = MOBA_HEADS, HEAD_DIM
    q = apply_rope((h @ w_q).reshape(B, S, H, Dh), cos, sin).transpose(0, 2, 1, 3)
    nb = kb.shape[2]
    topk = min(MOBA_TOPK, nb)
    nq = S // MOBA_Q_CHUNK
    q_chunks = q.reshape(B, H, nq, MOBA_Q_CHUNK, Dh).transpose(2, 0, 1, 3, 4)
    bi = jnp.arange(B)[:, None, None, None]
    hi = jnp.arange(H)[None, :, None, None]
    blk_ids = jnp.arange(nb)
    in_blk = jnp.arange(MOBA_BLOCK)
    scale = Dh ** -0.5

    def one_chunk(args):
        c, qc = args
        q0 = c * MOBA_Q_CHUNK
        qpos = q0 + jnp.arange(MOBA_Q_CHUNK)
        qblk = q0 // MOBA_BLOCK
        gate = jnp.einsum('bhqd,bhnd->bhqn', qc, kmean).astype(jnp.float32)
        gate = jnp.where(blk_ids < qblk, gate, -jnp.inf)
        _, idx = lax.top_k(gate, topk)
        valid = idx < qblk
        ksel = kb[bi, hi, idx]
        vsel = vb[bi, hi, idx]
        s_sel = jnp.einsum('bhqd,bhqjpd->bhqjp', qc, ksel).astype(jnp.float32) * scale
        s_sel = jnp.where(valid[..., None], s_sel, -jnp.inf)
        s_sel = s_sel.reshape(B, H, MOBA_Q_CHUNK, topk * MOBA_BLOCK)
        kown = lax.dynamic_index_in_dim(kb, qblk, axis=2, keepdims=False)
        vown = lax.dynamic_index_in_dim(vb, qblk, axis=2, keepdims=False)
        s_own = jnp.einsum('bhqd,bhpd->bhqp', qc, kown).astype(jnp.float32) * scale
        kpos = qblk * MOBA_BLOCK + in_blk
        s_own = jnp.where(kpos[None, :] <= qpos[:, None], s_own, -jnp.inf)
        p = jax.nn.softmax(jnp.concatenate([s_sel, s_own], axis=-1), axis=-1).astype(vb.dtype)
        p_sel = p[..., :topk * MOBA_BLOCK].reshape(B, H, MOBA_Q_CHUNK, topk, MOBA_BLOCK)
        p_own = p[..., topk * MOBA_BLOCK:]
        return (jnp.einsum('bhqjp,bhqjpd->bhqd', p_sel, vsel)
                + jnp.einsum('bhqp,bhpd->bhqd', p_own, vown))

    o = lax.map(one_chunk, (jnp.arange(nq), q_chunks))
    o = o.transpose(1, 0, 3, 2, 4).reshape(B, S, D_MODEL)
    return o @ w_o

def setup_inputs(seed: int = 0) -> dict:
    key = jax.random.key(seed)
    ks = jax.random.split(key, 16)
    f32 = jnp.float32
    nrm = lambda k, shape, s: jax.random.normal(k, shape, f32) * s
    gain = lambda k, shape: 1.0 + 0.05 * jax.random.normal(k, shape, f32)
    return {
        "x": jax.random.normal(ks[0], (BATCH, SEQ, D_MODEL), f32),
        "ffn_norm": gain(ks[1], (DEPTH, 2, 2, D_MODEL)),
        "ffn_w_in": nrm(ks[2], (DEPTH, 2, D_MODEL, 2 * D_FF), D_MODEL ** -0.5),
        "ffn_w_out": nrm(ks[3], (DEPTH, 2, D_FF, D_MODEL), D_FF ** -0.5),
        "mix_norm": gain(ks[4], (DEPTH, 2, D_MODEL)),
        "diff_w_qkv": nrm(ks[5], (N_A_LAYERS, D_MODEL, 3 * D_MODEL), D_MODEL ** -0.5),
        "diff_lambda": nrm(ks[6], (N_A_LAYERS, 4, HEAD_DIM), 0.1),
        "diff_subln": gain(ks[7], (N_A_LAYERS, 2 * HEAD_DIM)),
        "diff_w_o": nrm(ks[8], (N_A_LAYERS, D_MODEL, D_MODEL), D_MODEL ** -0.5),
        "kv_norm": gain(ks[9], (D_MODEL,)),
        "kv_w": nrm(ks[10], (D_MODEL, 2 * D_MODEL), D_MODEL ** -0.5),
        "moba_w_q": nrm(ks[11], (N_B_LAYERS, D_MODEL, D_MODEL), D_MODEL ** -0.5),
        "moba_w_o": nrm(ks[12], (N_B_LAYERS, D_MODEL, D_MODEL), D_MODEL ** -0.5),
    }

def reference(x, ffn_norm, ffn_w_in, ffn_w_out, mix_norm, diff_w_qkv, diff_lambda,
              diff_subln, diff_w_o, kv_norm, kv_w, moba_w_q, moba_w_o):
    S = x.shape[1]
    cos, sin = rope_tables(S, HEAD_DIM)
    kb = vb = kmean = None
    for l in range(DEPTH):
        if l == N_A_LAYERS:
            kb, vb, kmean = shared_kv(x, kv_norm, kv_w, cos, sin)
        x = macaron_half_ffn(x, ffn_norm[l, 0, 0], ffn_norm[l, 0, 1], ffn_w_in[l, 0], ffn_w_out[l, 0])
        h = rms_norm(x, mix_norm[l, 0])
        if l < N_A_LAYERS:
            lam_init = 0.8 - 0.6 * math.exp(-0.3 * l)
            y = diff_attention(h, diff_w_qkv[l], diff_lambda[l], diff_subln[l], diff_w_o[l],
                               lam_init, cos, sin)
        else:
            j = l - N_A_LAYERS
            y = moba_attention(h, moba_w_q[j], moba_w_o[j], kb, vb, kmean, cos, sin)
        x = x + rms_norm(y, mix_norm[l, 1])
        x = macaron_half_ffn(x, ffn_norm[l, 1, 0], ffn_norm[l, 1, 1], ffn_w_in[l, 1], ffn_w_out[l, 1])
    return x


_drawn_inputs = setup_inputs


def setup_inputs(seed=0):
    import zlib

    import numpy as np

    out = dict(_drawn_inputs(seed))
    spreads = {}
    factors = {}
    for name, (base, spread) in spreads.items():
        noise = np.random.default_rng([zlib.crc32(name.encode()), seed]).standard_normal(out[name].shape)
        drawn = base * np.exp(spread * noise) if base else spread * noise
        out[name] = __import__('jax').numpy.asarray(drawn.astype(out[name].dtype))
    for name, factor in factors.items():
        out[name] = (out[name] * factor).astype(out[name].dtype)
    return out
```

```python
from contextlib import ExitStack

import concourse.bass as bass
from concourse import mybir

F32 = mybir.dt.float32
F32R = mybir.dt.float32r
ALU = mybir.AluOpType
ACT = mybir.ActivationFunctionType

P = 128
D = 1024
SEQ = 256
TB = SEQ // P
KT = D // P
HEAD = 64
HALF = HEAD // 2
PAIRS = D // (2 * HEAD)
D_FF = 2816
FC = 256
FSTEPS = D_FF // FC
COLS = 512
EPS = 1e-6
LAM_INIT = 0.2
FLT_MAX = 3.4028234663852886e38
SCALE = HEAD ** -0.5

FFN, DIFF, MOBA = "ffn", "diff", "moba"
PHASES = [(FFN, (0, 0), 0.5), (DIFF, 0, 1.0), (FFN, (0, 1), 0.5),
          (FFN, (1, 0), 0.5), (MOBA, 0, 1.0), (FFN, (1, 1), 0.5)]
KV_BOUNDARY = 3
STEPS = [FSTEPS if k == FFN else PAIRS for k, _, _ in PHASES]


def turns_of(kind):
    return 3 * FSTEPS + 1 if kind == FFN else 3 * PAIRS + 2


TURN0 = [sum(turns_of(k) for k, _, _ in PHASES[:p]) for p in range(len(PHASES) + 1)]
STEP0 = [sum(STEPS[:p]) for p in range(len(PHASES) + 1)]
FSTEP0 = [sum(n for n, (k, _, _) in zip(STEPS[:p], PHASES) if k == FFN) for p in range(len(PHASES) + 1)]
PAIR0 = [sum(n for n, (k, _, _) in zip(STEPS[:p], PHASES) if k != FFN) for p in range(len(PHASES) + 1)]
ENTRY_DMAS = {FFN: 2, DIFF: 3, MOBA: 3}


def loads_before():
    have, out = [0, 0, 0], []
    for p, (kind, _, _) in enumerate(PHASES):
        out.append(list(have))
        a, b, c = slots(p)
        n = 16 * ENTRY_DMAS[kind] * STEPS[p]
        have[a] += n
        have[b] += n
        if kind == FFN:
            have[c] += 16 * (FSTEPS - 1)
            have[a] += 16
        else:
            have[c] += 16 * (PAIRS - 2)
            have[a] += 16
            have[b] += 16
    return out


def slots(p):
    return [(TURN0[p] + g) % 3 for g in range(3)]


LOADS0 = loads_before()

NORMS = [(0, "pre"), (1, "pre"), (2, "pre"), (KV_BOUNDARY, "kv"), (3, "pre"), (4, "pre"), (5, "pre")]


def norms_before(b):
    return sum(1 for x, _ in NORMS if x < b)


def build(nc, x, ffn_norm, ffn_w_in, ffn_w_out, mix_norm, diff_w_qkv, diff_lambda, diff_subln, diff_w_o,
          kv_norm, kv_w, moba_w_q, moba_w_o, rope_cos, rope_sin, out):
    with ExitStack() as ctx:
        def sb(name, shape, dt=F32):
            return ctx.enter_context(nc.sbuf_tensor(name, shape, dt))

        def psum(name, shape):
            return ctx.enter_context(nc.psum_tensor(name, shape, F32))

        def sem(name):
            return ctx.enter_context(nc.semaphore(name))

        w_raw = sb("w_raw", [P, 3, 4 * COLS])
        w_hi = sb("w_hi", [P, 3, 4 * COLS], F32R)
        w_lo = sb("w_lo", [P, 3, 4 * COLS], F32R)
        x_res = sb("x_res", [P, TB, D])
        h_row = sb("h_row", [P, TB, D])
        hT_hi = sb("hT_hi", [P, KT, SEQ], F32R)
        hT_lo = sb("hT_lo", [P, KT, SEQ], F32R)
        kvT_hi = sb("kvT_hi", [P, KT, SEQ], F32R)
        kvT_lo = sb("kvT_lo", [P, KT, SEQ], F32R)
        mT_hi = sb("mT_hi", [P, 2, SEQ], F32R)
        mT_lo = sb("mT_lo", [P, 2, SEQ], F32R)
        g_post = sb("g_post", [P, 2, D])
        g_pre = sb("g_pre", [P, 2, D])
        g_kv = sb("g_kv", [P, D])
        g_sub = sb("g_sub", [P, P])
        silu_g = sb("silu_g", [P, TB, FC])
        act_row = sb("act_row", [P, TB, FC])
        qk_row = sb("qk_row", [P, TB, 2 * P])
        v_row = sb("v_row", [P, TB, P])
        rope_u = sb("rope_u", [P, TB, 2 * P])
        rope_t = sb("rope_t", [P, TB, 2 * P])
        qk_rot = sb("qk_rot", [P, TB, 2 * P])
        qkT = sb("qkT", [P, 2, SEQ])
        prob = sb("prob", [P, 2, 3 * P])
        pT = sb("pT", [P, 2, 3 * P])
        o_raw = sb("o_raw", [P, TB, P])
        o_row = sb("o_row", [P, TB, P])
        cos_t = sb("cos_t", [P, TB, HALF])
        sin_t = sb("sin_t", [P, TB, HALF])
        causal = sb("causal", [P, 2 * P])
        ident = sb("ident", [P, P])
        lam_in = sb("lam_in", [P, 4 * HEAD])
        lam_pr = sb("lam_pr", [P, 2 * HEAD])
        lam_e = sb("lam_e", [P, 2])
        neg_lam = sb("neg_lam", [P, 1])
        minus_half = sb("minus_half", [P, 2])
        eps_sum = sb("eps_sum", [P, 2])
        wait_pad = sb("wait_pad", [P, 1])
        sq_sum = sb("sq_sum", [P, 4])
        rs = sb("rs", [P, 4])
        rs_tmp = sb("rs_tmp", [P, 4])
        row_max = sb("row_max", [P, 4])
        neg_max = sb("neg_max", [P, 4])
        row_sum = sb("row_sum", [P, 4])
        inv_sum = sb("inv_sum", [P, 4])
        mix_r = sb("mix_r", [P, 2])
        o_sq = sb("o_sq", [P, 2])
        o_ms = sb("o_ms", [P, 2])
        o_rs = sb("o_rs", [P, 2])

        entry = psum("entry", [P, TB, COLS])
        aux = psum("aux", [P, 2, COLS])
        y_acc = psum("y_acc", [P, TB, 2, COLS])
        turn_banks = [entry[:, :, :].rearrange("p b n -> p (b n)"), aux[:, :, :].rearrange("p b n -> p (b n)")]

        x_loaded = sem("x_loaded")
        gain_loaded = [sem("gain_loaded0"), sem("gain_loaded1")]
        kv_gain_loaded = sem("kv_gain_loaded")
        tables_loaded = sem("tables_loaded")
        w_loaded = [sem(f"w_loaded{i}") for i in range(3)]
        hi_made = sem("hi_made")
        lo_made = sem("lo_made")
        w_used = sem("w_used")
        consts_made = sem("consts_made")
        const_step = sem("const_step")
        lam_dot = sem("lam_dot")
        lam_exp = sem("lam_exp")
        lam_step = sem("lam_step")
        lam_made = sem("lam_made")
        y_squared = sem("y_squared")
        rs_step = sem("rs_step")
        y_rs_made = sem("y_rs_made")
        y_scaled = sem("y_scaled")
        x_updated = sem("x_updated")
        x_squared = sem("x_squared")
        x_rs_made = sem("x_rs_made")
        h_made = sem("h_made")
        h_turned = sem("h_turned")
        hT_hi_made = sem("hT_hi_made")
        hT_lo_made = sem("hT_lo_made")
        stored = sem("stored")
        silu_made = sem("silu_made")
        act_made = sem("act_made")
        qkv0_copied = sem("qkv0_copied")
        qkv1_copied = sem("qkv1_copied")
        rope_step = sem("rope_step")
        roped = sem("roped")
        qk_turned = sem("qk_turned")
        qkT_copied = sem("qkT_copied")
        scores_made = sem("scores_made")
        maxed = sem("maxed")
        neg_max_made = sem("neg_max_made")
        exp_made = sem("exp_made")
        inv_made = sem("inv_made")
        mix_made = sem("mix_made")
        prob_made = sem("prob_made")
        p_turned = sem("p_turned")
        pT_copied = sem("pT_copied")
        pv_made = sem("pv_made")
        o_divided = sem("o_divided")
        o_squared = sem("o_squared")
        o_ms_made = sem("o_ms_made")
        o_rs_made = sem("o_rs_made")
        o_made = sem("o_made")
        m_turned = sem("m_turned")
        mT_hi_made = sem("mT_hi_made")
        mT_lo_made = sem("mT_lo_made")

        block = ctx.enter_context(nc.Block())

        def width(kind, turn):
            if turn == "exit":
                return 2 * D if kind == FFN else D
            return 4 * (2 * FC if kind == FFN else 3 * P)

        @block.sync
        def _(sp):
            def load_gains(b):
                slot, n = b % 2, gain_loaded[b % 2]
                if b >= 2:
                    sp.wait_ge(h_made, 2 * norms_before(b - 1))
                if b > 0:
                    kind, w, _ = PHASES[b - 1]
                    g = ffn_norm[w[0], w[1], 1:2, :] if kind == FFN else mix_norm[0 if kind == DIFF else 1, 1:2, :]
                    sp.dma_start(g_post[:, slot, :], g.broadcast_to([P, D])).then_inc(n, 16)
                if b < len(PHASES):
                    kind, w, _ = PHASES[b]
                    g = ffn_norm[w[0], w[1], 0:1, :] if kind == FFN else mix_norm[0 if kind == DIFF else 1, 0:1, :]
                    sp.dma_start(g_pre[:, slot, :], g.broadcast_to([P, D])).then_inc(n, 16)

            def fill(turn, slot, dmas):
                if turn is not None:
                    sp.wait_ge(lo_made, turn - 2)
                for dst, src in dmas:
                    sp.dma_start(dst, src).then_inc(w_loaded[slot], 16)

            def entry_dmas(kind, w, slot, half, s):
                k = slice(4 * half, 4 * half + 4)
                dst = w_raw[:, slot, 0:width(kind, "entry")]
                if kind == FFN:
                    dst = dst.rearrange("p (k g n) -> p k g n", k=4, g=2)
                    src = ffn_w_in[w[0], w[1]].rearrange("(k p) (g n) -> p k g n", p=P, g=2)
                    return [(dst[:, :, g, :], src[:, k, g, bass.ds(s * FC, FC)]) for g in range(2)]
                dst = dst.rearrange("p (k g n) -> p k g n", k=4, g=3)
                if kind == DIFF:
                    src = diff_w_qkv[0].rearrange("(k p) (g n) -> p k g n", p=P, g=3)
                    return [(dst[:, :, g, :], src[:, k, g, bass.ds(s * P, P)]) for g in range(3)]
                q = moba_w_q[0].rearrange("(k p) n -> p k n", p=P)
                kv = kv_w.rearrange("(k p) (g n) -> p k g n", p=P, g=2)
                return [(dst[:, :, 0, :], q[:, k, bass.ds(s * P, P)])] + \
                       [(dst[:, :, 1 + g, :], kv[:, k, g, bass.ds(s * P, P)]) for g in range(2)]

            def exit_dmas(kind, w, slot, s):
                dst = w_raw[:, slot, 0:width(kind, "exit")]
                if kind == FFN:
                    src = ffn_w_out[w[0], w[1]].rearrange("(s k p) n -> p s k n", p=P, k=2)
                    return [(dst.rearrange("p (k n) -> p k n", k=2), src[:, bass.ds(s, 1), :, :].rearrange("p s k n -> p (s k) n"))]
                src = (diff_w_o if kind == DIFF else moba_w_o)[0].rearrange("(s p) n -> p s n", p=P)
                return [(dst.rearrange("p (s n) -> p s n", s=1), src[:, bass.ds(s, 1), :])]

            for t in range(TB):
                sp.dma_start(x_res[:, t, :], x[0, t * P:(t + 1) * P, :]).then_inc(x_loaded, 16)
            load_gains(0)
            for p, (kind, w, _) in enumerate(PHASES):
                a, b, c = slots(p)
                t0 = TURN0[p]
                lag = 1 if kind == FFN else 2
                for s in range(lag):
                    for half, slot in ((0, a), (1, b)):
                        turn = t0 + 3 * s + half
                        fill(turn if turn >= 3 else None, slot, entry_dmas(kind, w, slot, half, s))
                    if p == 0:
                        sp.dma_start(cos_t[:], rope_cos.rearrange("(t p) n -> p t n", p=P)).then_inc(tables_loaded, 16)
                        sp.dma_start(sin_t[:], rope_sin.rearrange("(t p) n -> p t n", p=P)).then_inc(tables_loaded, 16)
                        sp.dma_start(lam_in[:], diff_lambda.rearrange("a b c -> a (b c)").broadcast_to([P, 4 * HEAD])).then_inc(tables_loaded, 16)
                        sp.dma_start(g_sub[:], diff_subln.broadcast_to([P, P])).then_inc(tables_loaded, 16)
                        sp.dma_start(g_kv[:], kv_norm.rearrange("(a n) -> a n", a=1).broadcast_to([P, D])).then_inc(kv_gain_loaded, 16)
                load_gains(p + 1)
                with nc.sync.Fori(lag, STEPS[p]) as s:
                    fill(t0 + 3 * s, a, entry_dmas(kind, w, a, 0, s))
                    fill(t0 + 3 * s + 1, b, entry_dmas(kind, w, b, 1, s))
                    fill(t0 + 3 * s + 2, c, exit_dmas(kind, w, c, s - lag))
                for j in range(lag):
                    slot = (a, b)[j]
                    fill(t0 + 3 * STEPS[p] + j, slot, exit_dmas(kind, w, slot, STEPS[p] - lag + j))
            for t in range(TB):
                sp.wait_ge(x_updated, 2 * len(PHASES) - TB + 1 + t)
                sp.dma_start(out[0, t * P:(t + 1) * P, :], x_res[:, t, :]).then_inc(stored, 16)
            sp.wait_ge(stored, 16 * TB)

        @block.scalar
        def _(act):
            def split_hi(turn, slot, cols, loads, first=False, empty=False):
                act.wait_ge(w_loaded[slot], loads)
                if not first:
                    act.wait_ge(w_used, turn - 2)
                    act.wait_ge(lo_made, turn - 2)
                nc.scalar.activation(w_hi[:, slot, 0:cols], w_raw[:, slot, 0:cols], ACT.Copy)\
                    .then_inc(hi_made, 2 if empty else 1)

            def silu(g, used, first=False):
                act.wait_ge(w_used, used)
                if not first:
                    act.wait_ge(act_made, g)
                nc.scalar.activation(silu_g[:], entry[:, :, 0:FC], ACT.Silu).then_inc(silu_made, 1)

            def middle_hi(step, cols, used, bank):
                act.wait_ge(m_turned, step + 1)
                if used is not None:
                    act.wait_ge(w_used, used)
                n = cols // SEQ
                nc.scalar.activation(mT_hi[:, 0:n, :].rearrange("p k n -> p (k n)"), aux[:, bank, 0:cols], ACT.Copy)\
                    .then_inc(mT_hi_made, 1)

            def copy_qkv0(q, used):
                act.wait_ge(w_used, used)
                act.wait_ge(qkv0_copied, 2 * q)
                act.wait_ge(roped, q) if not isinstance(q, int) or q > 0 else None
                nc.scalar.activation(qk_row[:, 0, :], entry[:, 0, 0:2 * P], ACT.Copy).then_inc(qkv0_copied, 1)
                act.wait_ge(pv_made, q) if not isinstance(q, int) or q > 0 else None
                nc.scalar.activation(v_row[:, 0, :], entry[:, 0, 2 * P:3 * P], ACT.Copy).then_inc(qkv0_copied, 1)

            def copy_qkT(q):
                act.wait_ge(qk_turned, q + 1)
                nc.scalar.activation(qkT[:].rearrange("p a n -> p (a n)"), aux[:, 0, :], ACT.Copy).then_inc(qkT_copied, 1)

            def exps(q):
                act.wait_ge(neg_max_made, q + 1)
                for j in range(4):
                    sub, t = j // 2, j % 2
                    at = prob[:, sub, 0:P] if t == 0 else prob[:, sub, P:3 * P]
                    nc.scalar.activation(at, at, ACT.Exp, bias=neg_max[:, j:j + 1], scale=SCALE,
                                         accum_out=row_sum[:, j:j + 1]).then_inc(exp_made, 1)

            def copy_pT(q, kind):
                act.wait_ge(p_turned, q + 1)
                n = 1 if kind == DIFF else 2
                nc.scalar.activation(pT[:, 0:n, :], aux[:, 0:n, 0:3 * P], ACT.Copy).then_inc(pT_copied, 1)

            def boundary(b):
                v0 = 2 * norms_before(b)
                for t in range(TB if b > 0 else 0):
                    act.wait_ge(w_used, TURN0[b])
                    nc.scalar.activation(h_row[:, t, :], y_acc[:, t, :, :].rearrange("p a n -> p (a n)"), ACT.Square,
                                         accum_out=sq_sum[:, t:t + 1]).then_inc(y_squared, 1)
                if b == len(PHASES):
                    return
                for t in range(TB):
                    if b > 0:
                        act.wait_ge(x_updated, 2 * (b - 1) + t + 1)
                    else:
                        act.wait_ge(x_loaded, 32)
                    nc.scalar.activation(h_row[:, t, :], x_res[:, t, :], ACT.Square,
                                         accum_out=sq_sum[:, 2 + t:3 + t]).then_inc(x_squared, 1)
                for j, (_, which) in enumerate([n for n in NORMS if n[0] == b]):
                    hi = kvT_hi if which == "kv" else hT_hi
                    for t in range(TB):
                        act.wait_ge(h_turned, v0 + 2 * j + t + 1)
                        nc.scalar.activation(hi[:, :, t * P:(t + 1) * P],
                                             turn_banks[t].rearrange("p (k n) -> p k n", k=KT), ACT.Copy)\
                            .then_inc(hT_hi_made, 1)

            for p, (kind, w, _) in enumerate(PHASES):
                a, b, c = slots(p)
                la, lb, lc = LOADS0[p][a], LOADS0[p][b], LOADS0[p][c]
                t0, m0, f0, q0 = TURN0[p], STEP0[p], FSTEP0[p], PAIR0[p]
                wide, wexit, per = width(kind, "entry"), width(kind, "exit"), 16 * ENTRY_DMAS[kind]
                n = STEPS[p]
                if kind == FFN:
                    split_hi(t0, a, wide, la + per, first=(p == 0))
                    split_hi(t0 + 1, b, wide, lb + per, first=(p == 0), empty=True)
                    if p == 0:
                        boundary(0)

                    def ffn_step(s, first=False):
                        split_hi(t0 + 3 * s, a, wide, la + per * (s + 1))
                        silu(f0 + s - 1, t0 + 3 * s - 1, first and p == 0)
                        split_hi(t0 + 3 * s + 1, b, wide, lb + per * (s + 1))
                        middle_hi(m0 + s - 1, 2 * SEQ, None if first else t0 + 3 * s, 0)
                        split_hi(t0 + 3 * s + 2, c, wexit, lc + 16 * s)

                    ffn_step(1, first=True)
                    with nc.scalar.Fori(2, n) as s:
                        ffn_step(s)
                    split_hi(t0 + 3 * n, a, wexit, la + per * n + 16)
                    silu(f0 + n - 1, t0 + 3 * n - 1)
                    middle_hi(m0 + n - 1, 2 * SEQ, t0 + 3 * n, 0)
                else:
                    split_hi(t0, a, wide, la + per)
                    split_hi(t0 + 1, b, wide, lb + per, empty=True)
                    split_hi(t0 + 3, a, wide, la + 2 * per)
                    if p == 1:
                        act.wait_ge(lam_dot, 2)
                        nc.scalar.activation(lam_e[:], lam_e[:], ACT.Exp).then_inc(lam_exp, 1)
                    copy_qkv0(q0, t0 + 2)
                    split_hi(t0 + 4, b, wide, lb + 2 * per, empty=True)
                    copy_qkT(q0)
                    exps(q0)

                    def pair_step(s, first=False):
                        split_hi(t0 + 3 * s, a, wide, la + per * (s + 1))
                        copy_pT(q0 + s - 2, kind)
                        copy_qkv0(q0 + s - 1, t0 + 3 * s - 1)
                        split_hi(t0 + 3 * s + 1, b, wide, lb + per * (s + 1))
                        copy_qkT(q0 + s - 1)
                        split_hi(t0 + 3 * s + 2, c, wexit, lc + 16 * (s - 1))
                        middle_hi(m0 + s - 2, SEQ, None if first else t0 + 3 * s, 1)
                        exps(q0 + s - 1)

                    pair_step(2, first=True)
                    with nc.scalar.Fori(3, n) as s:
                        pair_step(s)
                    split_hi(t0 + 3 * n, a, wexit, la + per * n + 16)
                    copy_pT(q0 + n - 2, kind)
                    copy_qkv0(q0 + n - 1, t0 + 3 * n - 1)
                    split_hi(t0 + 3 * n + 1, b, wexit, lb + per * n + 16)
                    copy_qkT(q0 + n - 1)
                    middle_hi(m0 + n - 2, SEQ, t0 + 3 * n, 1)
                    exps(q0 + n - 1)
                    copy_pT(q0 + n - 1, kind)
                    middle_hi(m0 + n - 1, SEQ, t0 + 3 * n + 1, 1)
                boundary(p + 1)

        @block.vector
        def _(dve):
            def split_lo(turn, slot, cols, empty=False):
                dve.wait_ge(hi_made, turn + 1)
                nc.vector.tensor_tensor(w_lo[:, slot, 0:cols], w_raw[:, slot, 0:cols],
                                        w_hi[:, slot, 0:cols].bitcast(F32), ALU.subtract)\
                    .then_inc(lo_made, 2 if empty else 1)

            def gate(g, step, first=False):
                dve.wait_ge(silu_made, g + 1)
                if not first:
                    dve.wait_ge(m_turned, step)
                nc.vector.tensor_tensor(act_row[:], silu_g[:], entry[:, :, FC:2 * FC], ALU.mult).then_inc(act_made, 1)

            def middle_lo(step, cols, bank):
                dve.wait_ge(mT_hi_made, step + 1)
                n = cols // SEQ
                hi = mT_hi[:, 0:n, :].rearrange("p k n -> p (k n)")
                lo = mT_lo[:, 0:n, :].rearrange("p k n -> p (k n)")
                nc.vector.tensor_tensor(lo, aux[:, bank, 0:cols], hi.bitcast(F32), ALU.subtract).then_inc(mT_lo_made, 1)

            def copy_qkv1(q, used):
                dve.wait_ge(w_used, used)
                dve.wait_ge(roped, q) if not isinstance(q, int) or q > 0 else None
                dve.wait_ge(pv_made, q) if not isinstance(q, int) or q > 0 else None
                nc.vector.tensor_copy(qk_row[:, 1, :], entry[:, 1, 0:2 * P]).then_inc(qkv1_copied, 1)
                nc.vector.tensor_copy(v_row[:, 1, :], entry[:, 1, 2 * P:3 * P]).then_inc(qkv1_copied, 1)

            def masked_max(q):
                dve.wait_ge(scores_made, q + 1)
                dve.wait_ge(p_turned, q) if not isinstance(q, int) or q > 0 else None
                nc.vector.tensor_copy(wait_pad[:], causal[:, 0:1])
                for j in range(4):
                    sub, t = j // 2, j % 2
                    at = slice(0, P) if t == 0 else slice(P, 3 * P)
                    mask = causal[:, P:2 * P] if t == 0 else causal[:, :]
                    nc.vector.tensor_tensor_reduce(prob[:, sub, at], aux[:, sub, at], mask, 1.0, -FLT_MAX,
                                                   ALU.add, ALU.max, row_max[:, j:j + 1]).then_inc(maxed, 1)
                dve.wait_ge(maxed, 4 * q + 4)
                nc.vector.tensor_scalar(neg_max[:], row_max[:], -SCALE, None, ALU.mult).then_inc(neg_max_made, 1)

            def normalise(q, kind):
                dve.wait_ge(exp_made, 4 * q + 4)
                nc.vector.reciprocal(inv_sum[:], row_sum[:]).then_inc(inv_made, 1)
                if kind == DIFF:
                    dve.wait_ge(inv_made, q + 1)
                    nc.vector.scalar_tensor_tensor(out=mix_r[:], in0=row_sum[:, 0:2], scalar=neg_lam[:, 0:1],
                                                   in1=inv_sum[:, 2:4], op0=ALU.mult, op1=ALU.mult).then_inc(mix_made, 1)
                    dve.wait_ge(mix_made, q + 1)
                    for t, at in enumerate((slice(0, P), slice(P, 3 * P))):
                        nc.vector.scalar_tensor_tensor(out=prob[:, 0, at], in0=prob[:, 1, at], scalar=mix_r[:, t:t + 1],
                                                       in1=prob[:, 0, at], op0=ALU.mult, op1=ALU.add).then_inc(prob_made, 1)

            def norm_o(q, kind, turned):
                dve.wait_ge(pv_made, q + 1)
                dve.wait_ge(inv_made, q + 1)
                dve.wait_ge(m_turned, turned)
                o_ps = aux[:, 1, 0:2 * P]
                if kind == DIFF:
                    for t in range(TB):
                        nc.vector.tensor_scalar(o_raw[:, t, :], o_ps[:, t * P:(t + 1) * P], inv_sum[:, t:t + 1], None,
                                                ALU.mult).then_inc(o_divided, 1)
                    dve.wait_ge(o_divided, 2 * q + 2)
                    for t in range(TB):
                        nc.vector.tensor_tensor_reduce(o_row[:, t, :], o_raw[:, t, :], o_raw[:, t, :], 1.0, 0.0,
                                                       ALU.mult, ALU.add, o_sq[:, t:t + 1]).then_inc(o_squared, 1)
                    dve.wait_ge(o_rs_made, q + 1)
                    for t in range(TB):
                        nc.vector.scalar_tensor_tensor(out=o_row[:, t, :], in0=o_raw[:, t, :], scalar=o_rs[:, t:t + 1],
                                                       in1=g_sub[:], op0=ALU.mult, op1=ALU.mult).then_inc(o_made, 1)
                else:
                    for t in range(TB):
                        for sub in range(2):
                            at = slice(t * P + sub * HEAD, t * P + (sub + 1) * HEAD)
                            ins = nc.vector.tensor_scalar(o_row[:, t, sub * HEAD:(sub + 1) * HEAD], o_ps[:, at],
                                                          inv_sum[:, 2 * sub + t:2 * sub + t + 1], None, ALU.mult)
                        ins.then_inc(o_made, 1)

            def boundary(b):
                v0 = 2 * norms_before(b)
                slot = b % 2
                half = PHASES[b - 1][2] if b > 0 else None
                gains = 16 * sum((1 if x > 0 else 0) + (1 if x < len(PHASES) else 0) for x in range(slot, b + 1, 2))
                dve.wait_ge(gain_loaded[slot], gains)
                for t in range(TB if b > 0 else 0):
                    e = 2 * (b - 1) + t
                    dve.wait_ge(y_rs_made, e + 1)
                    nc.vector.scalar_tensor_tensor(out=h_row[:, t, :], in0=y_acc[:, t, :, :].rearrange("p a n -> p (a n)"),
                                                   scalar=rs[:, t:t + 1], in1=g_post[:, slot, :],
                                                   op0=ALU.mult, op1=ALU.mult).then_inc(y_scaled, 1)
                    dve.wait_ge(y_scaled, e + 1)
                    nc.vector.scalar_tensor_tensor(out=x_res[:, t, :], in0=h_row[:, t, :], scalar=half,
                                                   in1=x_res[:, t, :], op0=ALU.mult, op1=ALU.add).then_inc(x_updated, 1)
                if b == len(PHASES):
                    return
                for j, (_, which) in enumerate([n for n in NORMS if n[0] == b]):
                    lo, hi = (kvT_lo, kvT_hi) if which == "kv" else (hT_lo, hT_hi)
                    gain = g_kv[:] if which == "kv" else g_pre[:, slot, :]
                    if which == "kv":
                        dve.wait_ge(kv_gain_loaded, 16)
                    for t in range(TB):
                        v = v0 + 2 * j + t
                        dve.wait_ge(x_rs_made, 2 * b + t + 1)
                        if v >= 2:
                            dve.wait_ge(h_turned, v - 1)
                        nc.vector.scalar_tensor_tensor(out=h_row[:, t, :], in0=x_res[:, t, :], scalar=rs[:, 2 + t:3 + t],
                                                       in1=gain, op0=ALU.mult, op1=ALU.mult).then_inc(h_made, 1)
                    for t in range(TB):
                        dve.wait_ge(hT_hi_made, v0 + 2 * j + t + 1)
                        nc.vector.tensor_tensor(lo[:, :, t * P:(t + 1) * P], turn_banks[t].rearrange("p (k n) -> p k n", k=KT),
                                                hi[:, :, t * P:(t + 1) * P].bitcast(F32), ALU.subtract).then_inc(hT_lo_made, 1)

            for p, (kind, w, _) in enumerate(PHASES):
                a, b, c = slots(p)
                t0, m0, f0, q0 = TURN0[p], STEP0[p], FSTEP0[p], PAIR0[p]
                wide, wexit = width(kind, "entry"), width(kind, "exit")
                n = STEPS[p]
                split_lo(t0, a, wide)
                split_lo(t0 + 1, b, wide, empty=True)
                if p == 0:
                    boundary(0)
                if kind == FFN:
                    def ffn_step(s, first=False):
                        split_lo(t0 + 3 * s, a, wide)
                        gate(f0 + s - 1, m0 + s - 1, first and p == 0)
                        split_lo(t0 + 3 * s + 1, b, wide)
                        middle_lo(m0 + s - 1, 2 * SEQ, 0)
                        split_lo(t0 + 3 * s + 2, c, wexit)

                    ffn_step(1, first=True)
                    with nc.vector.Fori(2, n) as s:
                        ffn_step(s)
                    split_lo(t0 + 3 * n, a, wexit)
                    gate(f0 + n - 1, m0 + n - 1)
                    middle_lo(m0 + n - 1, 2 * SEQ, 0)
                else:
                    split_lo(t0 + 3, a, wide)
                    if p == 1:
                        dve.wait_ge(tables_loaded, 64)
                        for j in range(2):
                            at = 2 * j * HEAD
                            nc.vector.tensor_tensor_reduce(lam_pr[:, j * HEAD:(j + 1) * HEAD], lam_in[:, at:at + HEAD],
                                                           lam_in[:, at + HEAD:at + 2 * HEAD], 1.0, 0.0,
                                                           ALU.mult, ALU.add, lam_e[:, j:j + 1]).then_inc(lam_dot, 1)
                        nc.vector.tensor_scalar(g_sub[:], g_sub[:], (1.0 - LAM_INIT) * (2 * HEAD) ** 0.5, None, ALU.mult).then_inc(lam_step, 1)
                        dve.wait_ge(lam_exp, 1)
                        nc.vector.tensor_tensor(neg_lam[:], lam_e[:, 1:2], lam_e[:, 0:1], ALU.subtract).then_inc(lam_step, 1)
                        dve.wait_ge(lam_step, 2)
                        nc.vector.tensor_scalar(neg_lam[:], neg_lam[:], -LAM_INIT, None, ALU.add).then_inc(lam_made, 1)
                        dve.wait_ge(lam_made, 1)
                    copy_qkv1(q0, t0 + 2)
                    split_lo(t0 + 4, b, wide, empty=True)
                    masked_max(q0)
                    normalise(q0, kind)

                    def pair_step(s):
                        split_lo(t0 + 3 * s, a, wide)
                        copy_qkv1(q0 + s - 1, t0 + 3 * s - 1)
                        norm_o(q0 + s - 2, kind, m0 + s - 2)
                        split_lo(t0 + 3 * s + 1, b, wide)
                        split_lo(t0 + 3 * s + 2, c, wexit)
                        middle_lo(m0 + s - 2, SEQ, 1)
                        masked_max(q0 + s - 1)
                        normalise(q0 + s - 1, kind)

                    with nc.vector.Fori(2, n) as s:
                        pair_step(s)
                    split_lo(t0 + 3 * n, a, wexit)
                    copy_qkv1(q0 + n - 1, t0 + 3 * n - 1)
                    norm_o(q0 + n - 2, kind, m0 + n - 2)
                    split_lo(t0 + 3 * n + 1, b, wexit)
                    middle_lo(m0 + n - 2, SEQ, 1)
                    masked_max(q0 + n - 1)
                    normalise(q0 + n - 1, kind)
                    norm_o(q0 + n - 1, kind, m0 + n - 1)
                    middle_lo(m0 + n - 1, SEQ, 1)
                boundary(p + 1)

        @block.gpsimd
        def _(pool):
            nc.gpsimd.memset(ident[:], 0.0).then_inc(const_step, 1)
            nc.gpsimd.memset(causal[:], 0.0).then_inc(const_step, 1)
            nc.gpsimd.memset(minus_half[:], -0.5).then_inc(const_step, 1)
            nc.gpsimd.memset(eps_sum[:], 2 * HEAD * EPS).then_inc(const_step, 1)
            pool.wait_ge(const_step, 4)
            nc.gpsimd.affine_select(out=ident[:], in_=ident[:], compare_op=ALU.not_equal, fill=1.0, base=0,
                                    pattern=[[-1, P]], channel_multiplier=1).then_inc(consts_made, 1)
            nc.gpsimd.affine_select(out=causal[:, P:2 * P], in_=causal[:, P:2 * P], compare_op=ALU.is_ge, fill=-FLT_MAX,
                                    base=0, pattern=[[-1, P]], channel_multiplier=1).then_inc(consts_made, 1)

            def inverse_rms(dst, src, t, count, done, steps, out_sem):
                nc.gpsimd.tensor_scalar(rs_tmp[:, t:t + 1], src, 1.0 / count, EPS, ALU.mult, ALU.add).then_inc(rs_step, 1)
                pool.wait_ge(rs_step, steps)
                nc.gpsimd.tensor_tensor(dst, rs_tmp[:, t:t + 1], minus_half[:, 0:1], ALU.pow).then_inc(out_sem, 1)

            def boundary(b, steps):
                for t in range(TB if b > 0 else 0):
                    pool.wait_ge(y_squared, 2 * (b - 1) + t + 1)
                    steps += 1
                    inverse_rms(rs[:, t:t + 1], sq_sum[:, t:t + 1], t, D, None, steps, y_rs_made)
                if b == len(PHASES):
                    return steps
                for t in range(TB):
                    pool.wait_ge(x_squared, 2 * b + t + 1)
                    steps += 1
                    inverse_rms(rs[:, 2 + t:3 + t], sq_sum[:, 2 + t:3 + t], 2 + t, D, None, steps, x_rs_made)
                return steps

            def rope(q):
                pool.wait_ge(qkv0_copied, 2 * q + 2)
                pool.wait_ge(qkv1_copied, 2 * q + 2)
                pool.wait_ge(qk_turned, q) if not isinstance(q, int) or q > 0 else None
                for t in range(TB):
                    src = qk_row[:, t, :].rearrange("p (h a n) -> p h a n", a=2, n=HALF)
                    u = rope_u[:, t, :].rearrange("p (h a n) -> p h a n", a=2, n=HALF)
                    m = rope_t[:, t, :].rearrange("p (h a n) -> p h a n", a=2, n=HALF)
                    c = cos_t[:, t, :].rearrange("p (o n) -> p o n", o=1).broadcast_to([P, 8, HALF])
                    s = sin_t[:, t, :].rearrange("p (o n) -> p o n", o=1).broadcast_to([P, 4, HALF])
                    nc.gpsimd.tensor_tensor(u.rearrange("p h a n -> p (h a) n"), src.rearrange("p h a n -> p (h a) n"), c,
                                            ALU.mult).then_inc(rope_step, 1)
                    nc.gpsimd.tensor_tensor(m[:, :, 0, :], src[:, :, 1, :], s, ALU.mult).then_inc(rope_step, 1)
                    nc.gpsimd.tensor_tensor(m[:, :, 1, :], src[:, :, 0, :], s, ALU.mult).then_inc(rope_step, 1)
                pool.wait_ge(rope_step, 8 * q + 6)
                u = rope_u[:].rearrange("p t (h a n) -> p (t h) a n", a=2, n=HALF)
                m = rope_t[:].rearrange("p t (h a n) -> p (t h) a n", a=2, n=HALF)
                r = qk_rot[:].rearrange("p t (h a n) -> p (t h) a n", a=2, n=HALF)
                nc.gpsimd.tensor_tensor(r[:, :, 0, :], u[:, :, 0, :], m[:, :, 0, :], ALU.subtract).then_inc(rope_step, 1)
                nc.gpsimd.tensor_tensor(r[:, :, 1, :], u[:, :, 1, :], m[:, :, 1, :], ALU.add).then_inc(rope_step, 1)
                pool.wait_ge(rope_step, 8 * q + 8)
                nc.gpsimd.nop().then_inc(roped, 1)

            def o_norm(q):
                pool.wait_ge(o_squared, 2 * q + 2)
                nc.gpsimd.tensor_tensor(o_ms[:], o_sq[:], eps_sum[:], ALU.add).then_inc(o_ms_made, 1)
                pool.wait_ge(o_ms_made, q + 1)
                nc.gpsimd.tensor_tensor(o_rs[:], o_ms[:], minus_half[:], ALU.pow).then_inc(o_rs_made, 1)

            steps = boundary(0, 0)
            for p, (kind, _, _) in enumerate(PHASES):
                q0, n = PAIR0[p], STEPS[p]
                if kind == DIFF:
                    pool.wait_ge(tables_loaded, 64)
                    rope(q0)
                    with nc.gpsimd.Fori(1, n) as s:
                        rope(q0 + s)
                        o_norm(q0 + s - 1)
                    o_norm(q0 + n - 1)
                elif kind == MOBA:
                    with nc.gpsimd.Fori(0, n) as s:
                        rope(q0 + s)
                steps = boundary(p + 1, steps)

        @block.tensor
        def _(pe):
            pe.wait_ge(consts_made, 2)

            def three_passes(out_ap, hi, lo, whi, wlo, start, stop, grouped=True):
                nc.tensor.matmul(out_ap, hi, whi, start=start, stop=False, skip_group_check=not grouped)
                nc.tensor.matmul(out_ap, hi, wlo, start=False, stop=False, skip_group_check=not grouped)
                return nc.tensor.matmul(out_ap, lo, whi, start=False, stop=stop, skip_group_check=not grouped)

            def entry_tile(kind, slot, k):
                kk = k % 4
                n = width(kind, "entry") // 4
                whi = w_hi[:, slot, kk * n:(kk + 1) * n]
                wlo = w_lo[:, slot, kk * n:(kk + 1) * n]
                for t in range(TB):
                    tok = slice(t * P, (t + 1) * P)
                    if kind == MOBA:
                        three_passes(entry[:, t, 0:P], hT_hi[:, k, tok], hT_lo[:, k, tok], whi[:, 0:P], wlo[:, 0:P],
                                     k == 0, k == KT - 1, grouped=False)
                        last = three_passes(entry[:, t, P:n], kvT_hi[:, k, tok], kvT_lo[:, k, tok], whi[:, P:n], wlo[:, P:n],
                                            False, k == KT - 1, grouped=False)
                    else:
                        last = three_passes(entry[:, t, 0:n], hT_hi[:, k, tok], hT_lo[:, k, tok], whi, wlo,
                                            k == 0, k == KT - 1)
                return last

            def exit_product(kind, slot, step, turn, first, last_one, ks):
                pe.wait_ge(lo_made, turn + 1)
                pe.wait_ge(mT_lo_made, step + 1)
                for k in range(ks):
                    for t in range(TB):
                        tok = slice(t * P, (t + 1) * P)
                        for c in range(2):
                            at = slice(k * D + c * COLS, k * D + (c + 1) * COLS)
                            mm = three_passes(y_acc[:, t, c, :], mT_hi[:, k, tok], mT_lo[:, k, tok],
                                              w_hi[:, slot, at], w_lo[:, slot, at],
                                              first and k == 0, last_one and k == ks - 1)
                mm.then_inc(w_used, 1)

            def turn_act(g, step, first=False):
                pe.wait_ge(act_made, g + 1)
                if not first:
                    pe.wait_ge(mT_lo_made, step)
                for k in range(2):
                    for t in range(TB):
                        tr = nc.tensor.transpose(aux[:, 0, k * SEQ + t * P:k * SEQ + (t + 1) * P],
                                                 act_row[:, t, k * P:(k + 1) * P], ident[:])
                tr.then_inc(m_turned, 1)

            def turn_qk(q):
                pe.wait_ge(roped, q + 1)
                pe.wait_ge(pT_copied, q) if not isinstance(q, int) or q > 0 else None
                for j in range(2):
                    for t in range(TB):
                        tr = nc.tensor.transpose(aux[:, 0, j * SEQ + t * P:j * SEQ + (t + 1) * P],
                                                 qk_rot[:, t, j * P:(j + 1) * P], ident[:])
                tr.then_inc(qk_turned, 1)

            def turn_o(q, made):
                pe.wait_ge(o_made, made)
                for t in range(TB):
                    tr = nc.tensor.transpose(aux[:, 1, t * P:(t + 1) * P], o_row[:, t, :], ident[:])
                tr.then_inc(m_turned, 1)

            def scores(q, step=None):
                pe.wait_ge(qkT_copied, q + 1)
                if step is not None:
                    pe.wait_ge(mT_lo_made, step)
                for sub in range(2):
                    rows = slice(sub * HEAD, (sub + 1) * HEAD)
                    for t in range(TB):
                        at = slice(0, P) if t == 0 else slice(P, 3 * P)
                        mm = nc.tensor.matmul(aux[:, sub, at], qkT[rows, 0, t * P:(t + 1) * P],
                                              qkT[rows, 1, 0:(t + 1) * P], start=True, stop=True)
                mm.then_inc(scores_made, 1)

            def turn_p(q, kind):
                if kind == DIFF:
                    pe.wait_ge(prob_made, 2 * (q + 1))
                else:
                    pe.wait_ge(exp_made, 4 * (q + 1))
                for sub in range(1 if kind == DIFF else 2):
                    for j in range(3):
                        tr = nc.tensor.transpose(aux[:, sub, j * P:(j + 1) * P], prob[:, sub, j * P:(j + 1) * P], ident[:])
                tr.then_inc(p_turned, 1)

            def prob_v(q, kind):
                pe.wait_ge(pT_copied, q + 1)
                pe.wait_ge(qkv0_copied, 2 * q + 2)
                pe.wait_ge(qkv1_copied, 2 * q + 2)
                n = 2 * HEAD if kind == DIFF else HEAD
                for sub in range(1 if kind == DIFF else 2):
                    cols = slice(sub * HEAD, sub * HEAD + n)
                    for t in range(TB):
                        for kb in range(t + 1):
                            piece = t + kb
                            mm = nc.tensor.matmul(aux[:, 1, t * P + sub * HEAD:t * P + sub * HEAD + n],
                                                  pT[:, sub, piece * P:(piece + 1) * P], v_row[:, kb, cols],
                                                  start=(kb == 0), stop=(kb == t))
                mm.then_inc(pv_made, 1)

            def boundary(b):
                v0 = 2 * norms_before(b)
                for j in range(len([n for n in NORMS if n[0] == b])):
                    for t in range(TB):
                        v = v0 + 2 * j + t
                        pe.wait_ge(h_made, v + 1)
                        if v >= 2:
                            pe.wait_ge(hT_lo_made, v - 1)
                        for k in range(KT):
                            tr = nc.tensor.transpose(turn_banks[t][:, k * P:(k + 1) * P], h_row[:, t, k * P:(k + 1) * P], ident[:])
                        tr.then_inc(h_turned, 1)

            for p, (kind, w, _) in enumerate(PHASES):
                a, b, c = slots(p)
                t0, m0, f0, q0 = TURN0[p], STEP0[p], FSTEP0[p], PAIR0[p]
                n = STEPS[p]
                boundary(p)
                pe.wait_ge(hT_lo_made, 2 * norms_before(p + 1))

                def entry_half(s, half, between={}, empty=False):
                    slot = (a, b)[half]
                    pe.wait_ge(lo_made, t0 + 3 * s + half + 1)
                    for k in range(4 * half, 4 * half + 4):
                        for stage in between.get(k, ()):
                            stage()
                        mm = entry_tile(kind, slot, k)
                    mm.then_inc(w_used, 2 if empty else 1)

                if kind == FFN:
                    entry_half(0, 0)
                    entry_half(0, 1, empty=True)
                    turn_act(f0, m0, first=(p == 0))

                    def ffn_step(s, first=False):
                        pe.wait_ge(act_made, f0 + s)
                        entry_half(s, 0)
                        entry_half(s, 1)
                        exit_product(kind, c, m0 + s - 1, t0 + 3 * s + 2, first, False, 2)
                        turn_act(f0 + s, m0 + s)

                    ffn_step(1, first=True)
                    with nc.tensor.Fori(2, n) as s:
                        ffn_step(s)
                    exit_product(kind, a, m0 + n - 1, t0 + 3 * n, False, True, 2)
                else:
                    entry_half(0, 0)
                    entry_half(0, 1, empty=True)

                    def entry_free(s):
                        pe.wait_ge(qkv0_copied, 2 * (q0 + s))
                        pe.wait_ge(qkv1_copied, 2 * (q0 + s))

                    entry_free(1)
                    entry_half(1, 0, {1: [lambda: turn_qk(q0)], 2: [lambda: scores(q0)]})
                    entry_half(1, 1, {7: [lambda: turn_p(q0, kind)]}, empty=True)
                    prob_v(q0, kind)

                    def o_count(s):
                        return 2 * (q0 + s)

                    def pair_step(s, first=False):
                        entry_free(s)
                        entry_half(s, 0, {1: [lambda: turn_qk(q0 + s - 1)],
                                          2: [lambda: turn_o(q0 + s - 2, 2 * (q0 + s - 1))],
                                          3: [lambda: scores(q0 + s - 1, m0 + s - 1)]})
                        entry_half(s, 1, {7: [lambda: turn_p(q0 + s - 1, kind)]})
                        prob_v(q0 + s - 1, kind)
                        exit_product(kind, c, m0 + s - 2, t0 + 3 * s + 2, first, False, 1)

                    pair_step(2, first=True)
                    with nc.tensor.Fori(3, n) as s:
                        pair_step(s)
                    turn_qk(q0 + n - 1)
                    turn_o(q0 + n - 2, 2 * (q0 + n - 1))
                    scores(q0 + n - 1, m0 + n - 1)
                    exit_product(kind, a, m0 + n - 2, t0 + 3 * n, False, False, 1)
                    turn_p(q0 + n - 1, kind)
                    prob_v(q0 + n - 1, kind)
                    turn_o(q0 + n - 1, 2 * (q0 + n))
                    exit_product(kind, b, m0 + n - 1, t0 + 3 * n + 1, False, True, 1)


_INS = ["x", "ffn_norm", "ffn_w_in", "ffn_w_out", "mix_norm", "diff_w_qkv", "diff_lambda", "diff_subln", "diff_w_o",
        "kv_norm", "kv_w", "moba_w_q", "moba_w_o"]


def kernel(**inputs):
    import numpy as np
    import concourse.bacc as _bacc
    from concourse.bass_utils import run_bass_kernel_spmd as _run

    nc = _bacc.Bacc("TRN2", target_bir_lowering=False, num_devices=1)
    inv_freq = (1.0 / (np.float32(10000.0) ** (np.arange(0, HEAD, 2, dtype=np.float32) / np.float32(HEAD)))).astype(np.float32)
    angle = np.arange(SEQ, dtype=np.float32)[:, None] * inv_freq[None, :]
    arrays = {f"in_{n}": np.ascontiguousarray(inputs[n]) for n in _INS}
    arrays["in_rope_cos"] = np.cos(angle)
    arrays["in_rope_sin"] = np.sin(angle)
    args = [nc.dram_tensor(n, a.shape, mybir.dt.from_np(a.dtype), kind="ExternalInput").ap() for n, a in arrays.items()]
    args.append(nc.dram_tensor("out_0", (1, SEQ, D), F32, kind="ExternalOutput").ap())
    build(nc, *args)
    r = _run(nc, [arrays], core_ids=[0])
    return r.results[0]["out_0"]
```

```python
from contextlib import ExitStack

import concourse.bass as bass
from concourse import mybir

F32 = mybir.dt.float32
F32R = mybir.dt.float32r
BF16 = mybir.dt.bfloat16
ALU = mybir.AluOpType
ACT = mybir.ActivationFunctionType

P = 128
D = 1024
SEQ = 256
TB = SEQ // P
KT = D // P
HEAD = 64
HALF = HEAD // 2
PAIRS = D // (2 * HEAD)
D_FF = 2816
FC = 256
FSTEPS = D_FF // FC
COLS = 512
EPS = 1e-6
LAM_INIT = 0.2
FLT_MAX = 3.4028234663852886e38
SCALE = HEAD ** -0.5
RMS_ROOT = 32.0
assert RMS_ROOT ** 2 == D

FFN, DIFF, MOBA = "ffn", "diff", "moba"
PHASES = [(FFN, (0, 0), 0.5), (DIFF, 0, 1.0), (FFN, (0, 1), 0.5),
          (FFN, (1, 0), 0.5), (MOBA, 0, 1.0), (FFN, (1, 1), 0.5)]
NP = len(PHASES)
KV_PHASE = 3
STEPS = [FSTEPS if k == FFN else PAIRS for k, _, _ in PHASES]


def before(per_phase):
    return [sum(per_phase(k) for k, _, _ in PHASES[:p]) for p in range(NP + 1)]


TURN0 = before(lambda k: 3 * (FSTEPS if k == FFN else PAIRS))
MID0 = before(lambda k: FSTEPS - 1 if k == FFN else PAIRS - 2)
GATE0 = before(lambda k: FSTEPS + 1 if k == FFN else 0)
PAIR0 = before(lambda k: 0 if k == FFN else PAIRS)
FFN0 = before(lambda k: 1 if k == FFN else 0)
ENTRY_DMAS = {FFN: 2, DIFF: 3, MOBA: 3}
LOADS0 = [before(lambda k: 16 * ENTRY_DMAS[k] * (FSTEPS if k == FFN else PAIRS)),
          before(lambda k: 16 * ENTRY_DMAS[k] * (FSTEPS if k == FFN else PAIRS)),
          before(lambda k: 16 * (FSTEPS - 1 if k == FFN else PAIRS - 2))]


def positive(n):
    return not isinstance(n, int) or n > 0


def build(nc, x, ffn_norm, ffn_w_in, ffn_w_out, mix_norm, diff_w_qkv, diff_lambda, diff_subln, diff_w_o,
          kv_norm, kv_w, moba_w_q, moba_w_o, rope_cos, rope_sin, out):
    with ExitStack() as ctx:
        def sb(name, shape, dt=F32):
            return ctx.enter_context(nc.sbuf_tensor(name, shape, dt))

        def psum(name, shape):
            return ctx.enter_context(nc.psum_tensor(name, shape, F32))

        def sem(name):
            return ctx.enter_context(nc.semaphore(name))

        w_raw = sb("w_raw", [P, 4, 4 * COLS])
        w_hi = sb("w_hi", [P, 4, 4 * COLS], F32R)
        w_lo = sb("w_lo", [P, 4, 4 * COLS], F32R)
        TAIL = 3
        x_res = sb("x_res", [P, TB, D])
        h_row = sb("h_row", [P, TB, D])
        hT_hi = sb("hT_hi", [P, KT, SEQ], F32R)
        hT_lo = sb("hT_lo", [P, KT, SEQ], F32R)
        kvT_hi = sb("kvT_hi", [P, KT, SEQ], F32R)
        kvT_lo = sb("kvT_lo", [P, KT, SEQ], F32R)
        mT_hi = sb("mT_hi", [P, 2, SEQ], F32R)
        mT_lo = sb("mT_lo", [P, 2, SEQ], F32R)
        tT_hi = sb("tT_hi", [P, 2, SEQ], F32R)
        tT_lo = sb("tT_lo", [P, 2, SEQ], F32R)
        g_post = sb("g_post", [P, D])
        g_pre = sb("g_pre", [P, D])
        g_kv = sb("g_kv", [P, D])
        g_sub = sb("g_sub", [P, P])
        sq_out_y = sb("sq_out_y", [P, TB, D], BF16)
        sq_out_x = sb("sq_out_x", [P, TB, D], BF16)
        silu_g = sb("silu_g", [P, TB, FC])
        act_row = sb("act_row", [P, TB, FC])
        qk_row = sb("qk_row", [P, TB, 2 * P])
        v_row = sb("v_row", [P, TB, P])
        rope_u = sb("rope_u", [P, TB, 2 * P])
        rope_t = sb("rope_t", [P, TB, 2 * P])
        qk_rot = sb("qk_rot", [P, TB, 2 * P])
        qkT = sb("qkT", [P, 2, SEQ])
        prob = sb("prob", [P, 2, 3 * P])
        pT = sb("pT", [P, 2, 3 * P])
        o_raw = sb("o_raw", [P, TB, P])
        o_row = sb("o_row", [P, TB, P])
        cos_t = sb("cos_t", [P, TB, HALF])
        sin_t = sb("sin_t", [P, TB, HALF])
        causal = sb("causal", [P, 2 * P])
        ident = sb("ident", [P, P])
        lam_in = sb("lam_in", [P, 4 * HEAD])
        lam_pr = sb("lam_pr", [P, 2 * HEAD])
        lam_e = sb("lam_e", [P, 2])
        neg_lam = sb("neg_lam", [P, 1])
        minus_half = sb("minus_half", [P, 2])
        eps_sum = sb("eps_sum", [P, 2])
        wait_pad = sb("wait_pad", [P, 2])
        y_sq = sb("y_sq", [P, TB, 2])
        x_sq = sb("x_sq", [P, TB, 2])
        y_rs = sb("y_rs", [P, TB])
        x_rs = sb("x_rs", [P, TB])
        rs_tmp = sb("rs_tmp", [P, 2 * TB])
        row_max = sb("row_max", [P, 4])
        neg_max = sb("neg_max", [P, 4])
        row_sum = sb("row_sum", [P, 4])
        inv_sum = sb("inv_sum", [P, 4])
        mix_r = sb("mix_r", [P, 2])
        o_sq = sb("o_sq", [P, 2])
        o_ms = sb("o_ms", [P, 2])
        o_rs = sb("o_rs", [P, 2])

        entry = psum("entry", [P, TB, COLS])
        aux = psum("aux", [P, 2, COLS])
        y_acc = psum("y_acc", [P, TB, 2, COLS])

        x_loaded = [sem("x_loaded0"), sem("x_loaded1")]
        pre_loaded = sem("pre_loaded")
        post_loaded = sem("post_loaded")
        kv_gain_loaded = sem("kv_gain_loaded")
        tables_loaded = sem("tables_loaded")
        w_loaded = [sem(f"w_loaded{i}") for i in range(3)]
        tail_loaded = sem("tail_loaded")
        stored = sem("stored")
        hi_made = sem("hi_made")
        lo_made = sem("lo_made")
        w_used = sem("w_used")
        tail_hi_made = sem("tail_hi_made")
        tail_lo_made = sem("tail_lo_made")
        consts_made = sem("consts_made")
        const_step = sem("const_step")
        lam_dot = sem("lam_dot")
        lam_exp = sem("lam_exp")
        lam_step = sem("lam_step")
        lam_made = sem("lam_made")
        y_done = sem("y_done")
        y_squared = sem("y_squared")
        y_gained = sem("y_gained")
        y_rs_sum = sem("y_rs_sum")
        y_rs_made = sem("y_rs_made")
        x_updated = sem("x_updated")
        x_squared = sem("x_squared")
        x_rs_sum = sem("x_rs_sum")
        x_rs_made = sem("x_rs_made")
        h_made = sem("h_made")
        h_turned = sem("h_turned")
        hT_hi_made = sem("hT_hi_made")
        hT_lo_made = sem("hT_lo_made")
        kvh_made = sem("kvh_made")
        kv_turned = sem("kv_turned")
        kvT_hi_made = sem("kvT_hi_made")
        kvT_lo_made = sem("kvT_lo_made")
        entry0_done = sem("entry0_done")
        silu_made = sem("silu_made")
        act_made = sem("act_made")
        qkv0_copied = sem("qkv0_copied")
        qkv1_copied = sem("qkv1_copied")
        rope_prods = sem("rope_prods")
        roped = sem("roped")
        qk_turned = sem("qk_turned")
        qkT_copied = sem("qkT_copied")
        scores_made = sem("scores_made")
        maxed = sem("maxed")
        neg_max_made = sem("neg_max_made")
        exp_made = sem("exp_made")
        inv_made = sem("inv_made")
        mix_made = sem("mix_made")
        prob_made = sem("prob_made")
        p_turned = sem("p_turned")
        pT_copied = sem("pT_copied")
        pv_made = sem("pv_made")
        o_divided = sem("o_divided")
        o_squared = sem("o_squared")
        o_ms_made = sem("o_ms_made")
        o_rs_made = sem("o_rs_made")
        o_made = sem("o_made")
        m_turned = sem("m_turned")
        mT_hi_made = sem("mT_hi_made")
        mT_lo_made = sem("mT_lo_made")
        t_turned = sem("t_turned")
        tT_hi_made = sem("tT_hi_made")
        tT_lo_made = sem("tT_lo_made")

        block = ctx.enter_context(nc.Block())

        def entry_width(kind):
            return 2 * FC if kind == FFN else 3 * P

        def exit_cols(kind):
            return 2 * D if kind == FFN else D

        def turn_banks(t, half):
            return (entry, aux)[t][:, half, :]

        @block.sync
        def _(sp):
            def gain_row(p, which):
                kind, w, _ = PHASES[p]
                return ffn_norm[w[0], w[1], which:which + 1, :] if kind == FFN else \
                    mix_norm[0 if kind == DIFF else 1, which:which + 1, :]

            def load_pre(p):
                if p > 0:
                    sp.wait_ge(h_made, 4 * p)
                sp.dma_start(g_pre[:], gain_row(p, 0).broadcast_to([P, D])).then_inc(pre_loaded, 16)

            def load_post(p):
                if p > 0:
                    sp.wait_ge(y_gained, 4 * p)
                sp.dma_start(g_post[:], gain_row(p, 1).broadcast_to([P, D])).then_inc(post_loaded, 16)

            def fill(turn, slot, dmas):
                if turn is not None:
                    sp.wait_ge(lo_made, turn - 2)
                for dst, src in dmas:
                    sp.dma_start(dst, src).then_inc(w_loaded[slot], 16)

            def entry_dmas(kind, w, half, s):
                k = slice(4 * half, 4 * half + 4)
                dst = w_raw[:, half, 0:4 * entry_width(kind)]
                if kind == FFN:
                    dst = dst.rearrange("p (k g n) -> p k g n", k=4, g=2)
                    src = ffn_w_in[w[0], w[1]].rearrange("(k p) (g n) -> p k g n", p=P, g=2)
                    return [(dst[:, :, g, :], src[:, k, g, bass.ds(s * FC, FC)]) for g in range(2)]
                dst = dst.rearrange("p (k g n) -> p k g n", k=4, g=3)
                if kind == DIFF:
                    src = diff_w_qkv[0].rearrange("(k p) (g n) -> p k g n", p=P, g=3)
                    return [(dst[:, :, g, :], src[:, k, g, bass.ds(s * P, P)]) for g in range(3)]
                q = moba_w_q[0].rearrange("(k p) n -> p k n", p=P)
                kv = kv_w.rearrange("(k p) (g n) -> p k g n", p=P, g=2)
                return [(dst[:, :, 0, :], q[:, k, bass.ds(s * P, P)])] + \
                       [(dst[:, :, 1 + g, :], kv[:, k, g, bass.ds(s * P, P)]) for g in range(2)]

            def exit_rows(kind, w):
                return ffn_w_out[w[0], w[1]] if kind == FFN else (diff_w_o if kind == DIFF else moba_w_o)[0]

            def exit_dmas(kind, w, s):
                ks = exit_cols(kind) // D
                src = exit_rows(kind, w).rearrange("(s k p) n -> p s k n", p=P, k=ks)[:, bass.ds(s, 1), :, :]
                dst = w_raw[:, 2, 0:ks * D].rearrange("p (k n) -> p k n", k=ks)
                return [(dst, src.rearrange("p s k n -> p (s k) n"))]

            sp.dma_start(x_res[:, 0, :], x[0, 0:P, :]).then_inc(x_loaded[0], 16)
            load_pre(0)
            sp.dma_start(x_res[:, 1, :], x[0, P:2 * P, :]).then_inc(x_loaded[1], 16)
            for p, (kind, w, _) in enumerate(PHASES):
                t0 = TURN0[p]
                lag = 1 if kind == FFN else 2
                for s in range(lag):
                    for half in range(2):
                        turn = t0 + 3 * s + half
                        fill(turn if turn >= 3 else None, half, entry_dmas(kind, w, half, s))
                if p == 0:
                    sp.dma_start(g_kv[:], kv_norm.rearrange("(a n) -> a n", a=1).broadcast_to([P, D])).then_inc(kv_gain_loaded, 16)
                    sp.dma_start(cos_t[:], rope_cos.rearrange("(t p) n -> p t n", p=P)).then_inc(tables_loaded, 16)
                    sp.dma_start(sin_t[:], rope_sin.rearrange("(t p) n -> p t n", p=P)).then_inc(tables_loaded, 16)
                    sp.dma_start(lam_in[:], diff_lambda.rearrange("a b c -> a (b c)").broadcast_to([P, 4 * HEAD])).then_inc(tables_loaded, 16)
                    sp.dma_start(g_sub[:], diff_subln.broadcast_to([P, P])).then_inc(tables_loaded, 16)
                with nc.sync.Fori(lag, lag + 2) as s:
                    fill(t0 + 3 * s, 0, entry_dmas(kind, w, 0, s))
                    fill(t0 + 3 * s + 1, 1, entry_dmas(kind, w, 1, s))
                    fill(t0 + 3 * s + 2, 2, exit_dmas(kind, w, s - lag))
                load_post(p)
                if p + 1 < NP:
                    load_pre(p + 1)
                if p > 0:
                    sp.wait_ge(tail_lo_made, p)
                sp.dma_start(w_raw[:, TAIL, :].rearrange("p (k n) -> p k n", k=2),
                             exit_rows(kind, w).rearrange("(k p) n -> p k n", p=P)[:, -2:, :]).then_inc(tail_loaded, 16)
                with nc.sync.Fori(lag + 2, STEPS[p]) as s:
                    fill(t0 + 3 * s, 0, entry_dmas(kind, w, 0, s))
                    fill(t0 + 3 * s + 1, 1, entry_dmas(kind, w, 1, s))
                    fill(t0 + 3 * s + 2, 2, exit_dmas(kind, w, s - lag))
            for t in range(TB):
                sp.wait_ge(x_updated, 4 * (NP - 1) + 2 * t + 2)
                sp.dma_start(out[0, t * P:(t + 1) * P, :], x_res[:, t, :]).then_inc(stored, 16)
            sp.wait_ge(stored, 16 * TB)

        @block.scalar
        def _(act):
            def split_hi(p, turn, slot, cols, loads, empty=False):
                act.wait_ge(w_loaded[slot], loads)
                if not isinstance(turn, int) or turn >= 3:
                    act.wait_ge(w_used, turn - 2)
                    act.wait_ge(lo_made, turn - 2)
                nc.scalar.activation(w_hi[:, slot, 0:cols], w_raw[:, slot, 0:cols], ACT.Copy)\
                    .then_inc(hi_made, 2 if empty else 1)

            def entry_hi(p, s, half, empty=False):
                kind = PHASES[p][0]
                split_hi(p, TURN0[p] + 3 * s + half, half, 4 * entry_width(kind),
                         LOADS0[half][p] + 16 * ENTRY_DMAS[kind] * (s + 1), empty)

            def exit_hi(p, s):
                kind = PHASES[p][0]
                lag = 1 if kind == FFN else 2
                split_hi(p, TURN0[p] + 3 * s + 2, 2, exit_cols(kind), LOADS0[2][p] + 16 * (s - lag + 1))

            def tail_hi(p):
                act.wait_ge(tail_loaded, 16 * (p + 1))
                if p > 0:
                    act.wait_ge(y_done, 2 * p)
                nc.scalar.activation(w_hi[:, TAIL, :], w_raw[:, TAIL, :], ACT.Copy).then_inc(tail_hi_made, 1)

            def silu(g, used):
                act.wait_ge(w_used, used)
                if positive(g):
                    act.wait_ge(act_made, g)
                nc.scalar.activation(silu_g[:], entry[:, :, 0:FC], ACT.Silu).then_inc(silu_made, 1)

            def silu_block(p, t):
                if t == 0:
                    act.wait_ge(entry0_done, FFN0[p] + 1)
                else:
                    act.wait_ge(w_used, TURN0[p + 1] - 1)
                act.wait_ge(act_made, GATE0[p] + FSTEPS - 1 + t)
                nc.scalar.activation(silu_g[:, t, :], entry[:, t, 0:FC], ACT.Silu).then_inc(silu_made, 1)

            def middle_hi(m, cols, bank, used=None):
                act.wait_ge(m_turned, m + 1)
                if used is not None:
                    act.wait_ge(w_used, used)
                nc.scalar.activation(mT_hi[:, 0:cols // SEQ, :].rearrange("p k n -> p (k n)"), aux[:, bank, 0:cols],
                                     ACT.Copy).then_inc(mT_hi_made, 1)

            def tail_piece(buf, kind, i):
                return buf[:, :, i * P:(i + 1) * P] if kind == FFN else buf[:, i:i + 1, :]

            def tail_middle_hi(p, i):
                kind = PHASES[p][0]
                act.wait_ge(t_turned, 2 * p + i + 1)
                src = aux[:, i if kind == FFN else 1, 0:SEQ].rearrange("p (k n) -> p k n", k=2 if kind == FFN else 1)
                nc.scalar.activation(tail_piece(tT_hi, kind, i), src, ACT.Copy).then_inc(tT_hi_made, 1)

            def copy_qkv0(q, used):
                act.wait_ge(w_used, used)
                if positive(q):
                    act.wait_ge(roped, 2 * q)
                    act.wait_ge(pv_made, q)
                nc.scalar.activation(qk_row[:, 0, :], entry[:, 0, 0:2 * P], ACT.Copy).then_inc(qkv0_copied, 1)
                nc.scalar.activation(v_row[:, 0, :], entry[:, 0, 2 * P:3 * P], ACT.Copy).then_inc(qkv0_copied, 1)

            def copy_qkT(q):
                act.wait_ge(qk_turned, q + 1)
                nc.scalar.activation(qkT[:].rearrange("p a n -> p (a n)"), aux[:, 0, :], ACT.Copy).then_inc(qkT_copied, 1)

            def exps(q):
                for sub in range(2):
                    act.wait_ge(neg_max_made, 2 * q + sub + 1)
                    for t in range(TB):
                        j = 2 * sub + t
                        at = prob[:, sub, 0:P] if t == 0 else prob[:, sub, P:3 * P]
                        nc.scalar.activation(at, at, ACT.Exp, bias=neg_max[:, j:j + 1], scale=SCALE,
                                             accum_out=row_sum[:, j:j + 1]).then_inc(exp_made, 1)

            def copy_pT(q, kind):
                act.wait_ge(p_turned, q + 1)
                n = 1 if kind == DIFF else 2
                nc.scalar.activation(pT[:, 0:n, :], aux[:, 0:n, 0:3 * P], ACT.Copy).then_inc(pT_copied, 1)

            def square_y(p, t):
                act.wait_ge(y_done, 2 * p + t + 1)
                for half in range(2):
                    if half == 1:
                        act.wait_ge(y_gained, 4 * p + 2 * t + 1)
                    nc.scalar.activation(sq_out_y[:, t, half * COLS:(half + 1) * COLS], y_acc[:, t, half, :], ACT.Square,
                                         accum_out=y_sq[:, t, half:half + 1]).then_inc(y_squared, 1)

            def square_x(b, t):
                for half in range(2):
                    if b > 0:
                        act.wait_ge(x_updated, 4 * (b - 1) + 2 * t + half + 1)
                    else:
                        act.wait_ge(x_loaded[t], 16)
                    at = slice(half * COLS, (half + 1) * COLS)
                    nc.scalar.activation(sq_out_x[:, t, at], x_res[:, t, at], ACT.Square,
                                         accum_out=x_sq[:, t, half:half + 1]).then_inc(x_squared, 1)

            def turned_hi(b, t):
                for half in range(2):
                    act.wait_ge(h_turned, 4 * b + 2 * t + half + 1)
                    nc.scalar.activation(hT_hi[:, 4 * half:4 * half + 4, t * P:(t + 1) * P],
                                         turn_banks(t, half).rearrange("p (k n) -> p k n", k=4), ACT.Copy,
                                         scale=RMS_ROOT).then_inc(hT_hi_made, 1)

            def kv_hi(i):
                t, half = i // 2, i % 2
                act.wait_ge(kv_turned, i + 1)
                nc.scalar.activation(kvT_hi[:, 4 * half:4 * half + 4, t * P:(t + 1) * P],
                                     aux[:, 1, :].rearrange("p (k n) -> p k n", k=4), ACT.Copy,
                                     scale=RMS_ROOT).then_inc(kvT_hi_made, 1)

            square_x(0, 0)
            square_x(0, 1)
            entry_hi(0, 0, 0)
            turned_hi(0, 0)
            entry_hi(0, 0, 1, empty=True)
            turned_hi(0, 1)
            for p, (kind, w, _) in enumerate(PHASES):
                t0, m0, g0, q0, n = TURN0[p], MID0[p], GATE0[p], PAIR0[p], STEPS[p]
                if kind == FFN:
                    def ffn_step(s, first=False):
                        entry_hi(p, s, 0)
                        silu(g0 + s - 1, t0 + 3 * s - 1)
                        entry_hi(p, s, 1)
                        middle_hi(m0 + s - 1, 2 * SEQ, 0, None if first else t0 + 3 * s)
                        exit_hi(p, s)

                    if p == KV_PHASE:
                        kv_hi(0)
                        entry_hi(p, 1, 0)
                        silu(g0, t0 + 2)
                        kv_hi(1)
                        entry_hi(p, 1, 1)
                        middle_hi(m0, 2 * SEQ, 0)
                        exit_hi(p, 1)
                        kv_hi(2)
                        kv_hi(3)
                    else:
                        ffn_step(1, first=True)
                    with nc.scalar.Fori(2, n) as s:
                        ffn_step(s)
                    tail_hi(p)
                    silu_block(p, 0)
                    tail_middle_hi(p, 0)
                    if p + 1 < NP:
                        entry_hi(p + 1, 0, 0)
                    square_y(p, 0)
                    silu_block(p, 1)
                    if p + 1 < NP:
                        square_x(p + 1, 0)
                    tail_middle_hi(p, 1)
                    if p + 1 < NP:
                        entry_hi(p + 1, 0, 1, empty=True)
                        turned_hi(p + 1, 0)
                    square_y(p, 1)
                    if p + 1 < NP:
                        square_x(p + 1, 1)
                        turned_hi(p + 1, 1)
                else:
                    entry_hi(p, 1, 0)
                    if kind == DIFF:
                        act.wait_ge(lam_dot, 2)
                        nc.scalar.activation(lam_e[:], lam_e[:], ACT.Exp).then_inc(lam_exp, 1)
                    copy_qkv0(q0, t0 + 2)
                    entry_hi(p, 1, 1, empty=True)
                    copy_qkT(q0)
                    exps(q0)

                    def pair_step(s, first=False):
                        entry_hi(p, s, 0)
                        if first:
                            copy_pT(q0 + s - 2, kind)
                            copy_qkv0(q0 + s - 1, t0 + 3 * s - 1)
                        else:
                            copy_qkv0_then_pT(s)
                        entry_hi(p, s, 1)
                        exit_hi(p, s)
                        middle_hi(m0 + s - 2, SEQ, 1, None if first else t0 + 3 * s)
                        copy_qkT(q0 + s - 1)
                        exps(q0 + s - 1)

                    def copy_qkv0_then_pT(s):
                        copy_pT(q0 + s - 2, kind)
                        copy_qkv0(q0 + s - 1, t0 + 3 * s - 1)

                    pair_step(2, first=True)
                    with nc.scalar.Fori(3, n) as s:
                        pair_step(s)
                    tail_hi(p)
                    copy_pT(q0 + n - 2, kind)
                    copy_qkv0(q0 + n - 1, t0 + 3 * n - 1)
                    tail_middle_hi(p, 0)
                    copy_qkT(q0 + n - 1)
                    exps(q0 + n - 1)
                    entry_hi(p + 1, 0, 0)
                    copy_pT(q0 + n - 1, kind)
                    tail_middle_hi(p, 1)
                    square_y(p, 0)
                    square_y(p, 1)
                    square_x(p + 1, 0)
                    square_x(p + 1, 1)
                    entry_hi(p + 1, 0, 1, empty=True)
                    turned_hi(p + 1, 0)
                    turned_hi(p + 1, 1)

        @block.vector
        def _(dve):
            def split_lo(turn, slot, cols, empty=False):
                dve.wait_ge(hi_made, turn + 1)
                nc.vector.tensor_tensor(w_lo[:, slot, 0:cols], w_raw[:, slot, 0:cols],
                                        w_hi[:, slot, 0:cols].bitcast(F32), ALU.subtract)\
                    .then_inc(lo_made, 2 if empty else 1)

            def entry_lo(p, s, half, empty=False):
                split_lo(TURN0[p] + 3 * s + half, half, 4 * entry_width(PHASES[p][0]), empty)

            def exit_lo(p, s):
                split_lo(TURN0[p] + 3 * s + 2, 2, exit_cols(PHASES[p][0]))

            def tail_lo(p):
                dve.wait_ge(tail_hi_made, p + 1)
                nc.vector.tensor_tensor(w_lo[:, TAIL, :], w_raw[:, TAIL, :], w_hi[:, TAIL, :].bitcast(F32), ALU.subtract)\
                    .then_inc(tail_lo_made, 1)

            def gate(g, m):
                dve.wait_ge(silu_made, g + 1)
                if positive(m):
                    dve.wait_ge(m_turned, m)
                nc.vector.tensor_tensor(act_row[:], silu_g[:], entry[:, :, FC:2 * FC], ALU.mult).then_inc(act_made, 1)

            def gate_block(p, t):
                dve.wait_ge(silu_made, GATE0[p] + FSTEPS + t)
                dve.wait_ge(m_turned, MID0[p + 1])
                nc.vector.tensor_tensor(act_row[:, t, :], silu_g[:, t, :], entry[:, t, FC:2 * FC], ALU.mult)\
                    .then_inc(act_made, 1)

            def middle_lo(m, cols, bank):
                dve.wait_ge(mT_hi_made, m + 1)
                k = cols // SEQ
                nc.vector.tensor_tensor(mT_lo[:, 0:k, :].rearrange("p k n -> p (k n)"), aux[:, bank, 0:cols],
                                        mT_hi[:, 0:k, :].rearrange("p k n -> p (k n)").bitcast(F32), ALU.subtract)\
                    .then_inc(mT_lo_made, 1)

            def tail_piece(buf, kind, i):
                return buf[:, :, i * P:(i + 1) * P] if kind == FFN else buf[:, i:i + 1, :]

            def tail_middle_lo(p, i):
                kind = PHASES[p][0]
                dve.wait_ge(tT_hi_made, 2 * p + i + 1)
                src = aux[:, i if kind == FFN else 1, 0:SEQ].rearrange("p (k n) -> p k n", k=2 if kind == FFN else 1)
                nc.vector.tensor_tensor(tail_piece(tT_lo, kind, i), src, tail_piece(tT_hi, kind, i).bitcast(F32),
                                        ALU.subtract).then_inc(tT_lo_made, 1)

            def copy_qkv1(q, used):
                dve.wait_ge(w_used, used)
                if positive(q):
                    dve.wait_ge(roped, 2 * q)
                    dve.wait_ge(pv_made, q)
                nc.vector.tensor_copy(qk_row[:, 1, :], entry[:, 1, 0:2 * P]).then_inc(qkv1_copied, 1)
                nc.vector.tensor_copy(v_row[:, 1, :], entry[:, 1, 2 * P:3 * P]).then_inc(qkv1_copied, 1)

            def masked_max(q):
                dve.wait_ge(scores_made, q + 1)
                if positive(q):
                    dve.wait_ge(p_turned, q)
                nc.vector.tensor_copy(wait_pad[:, 0:1], causal[:, 0:1])
                for sub in range(2):
                    for t in range(TB):
                        j = 2 * sub + t
                        at = slice(0, P) if t == 0 else slice(P, 3 * P)
                        mask = causal[:, P:2 * P] if t == 0 else causal[:, :]
                        nc.vector.tensor_tensor_reduce(prob[:, sub, at], aux[:, sub, at], mask, 1.0, -FLT_MAX,
                                                       ALU.add, ALU.max, row_max[:, j:j + 1]).then_inc(maxed, 1)
                    dve.wait_ge(maxed, 4 * q + 2 * sub + 2)
                    nc.vector.tensor_scalar(neg_max[:, 2 * sub:2 * sub + 2], row_max[:, 2 * sub:2 * sub + 2], -SCALE, None,
                                            ALU.mult).then_inc(neg_max_made, 1)

            def normalise(q, kind):
                dve.wait_ge(exp_made, 4 * q + 4)
                nc.vector.reciprocal(inv_sum[:], row_sum[:]).then_inc(inv_made, 1)
                if kind == DIFF:
                    dve.wait_ge(inv_made, q + 1)
                    nc.vector.scalar_tensor_tensor(out=mix_r[:], in0=row_sum[:, 0:2], scalar=neg_lam[:, 0:1],
                                                   in1=inv_sum[:, 2:4], op0=ALU.mult, op1=ALU.mult).then_inc(mix_made, 1)
                    dve.wait_ge(mix_made, q + 1)
                    for t, at in enumerate((slice(0, P), slice(P, 3 * P))):
                        nc.vector.scalar_tensor_tensor(out=prob[:, 0, at], in0=prob[:, 1, at], scalar=mix_r[:, t:t + 1],
                                                       in1=prob[:, 0, at], op0=ALU.mult, op1=ALU.add).then_inc(prob_made, 1)

            def divide_o(q, kind, made):
                dve.wait_ge(pv_made, q + 1)
                dve.wait_ge(inv_made, q + 1)
                if made is not None:
                    dve.wait_ge(*made)
                o_ps = aux[:, 1, 0:2 * P]
                if kind == DIFF:
                    for t in range(TB):
                        nc.vector.tensor_scalar(o_raw[:, t, :], o_ps[:, t * P:(t + 1) * P], inv_sum[:, t:t + 1], None,
                                                ALU.mult).then_inc(o_divided, 1)
                    dve.wait_ge(o_divided, 2 * q + 2)
                    for t in range(TB):
                        nc.vector.tensor_tensor_reduce(o_row[:, t, :], o_raw[:, t, :], o_raw[:, t, :], 1.0, 0.0,
                                                       ALU.mult, ALU.add, o_sq[:, t:t + 1]).then_inc(o_squared, 1)
                else:
                    for t in range(TB):
                        for sub in range(2):
                            at = slice(t * P + sub * HEAD, t * P + (sub + 1) * HEAD)
                            ins = nc.vector.tensor_scalar(o_row[:, t, sub * HEAD:(sub + 1) * HEAD], o_ps[:, at],
                                                          inv_sum[:, 2 * sub + t:2 * sub + t + 1], None, ALU.mult)
                        ins.then_inc(o_made, 1)

            def norm_o(q, kind):
                if kind == DIFF:
                    dve.wait_ge(o_rs_made, q + 1)
                    for t in range(TB):
                        nc.vector.scalar_tensor_tensor(out=o_row[:, t, :], in0=o_raw[:, t, :], scalar=o_rs[:, t:t + 1],
                                                       in1=g_sub[:], op0=ALU.mult, op1=ALU.mult).then_inc(o_made, 1)

            def gain_y(p, t):
                dve.wait_ge(post_loaded, 16 * (p + 1))
                dve.wait_ge(y_done, 2 * p + t + 1)
                for half in (1, 0):
                    at = slice(half * COLS, (half + 1) * COLS)
                    if half == 0:
                        dve.wait_ge(y_squared, 4 * p + 2 * t + 1)
                    nc.vector.scalar_tensor_tensor(out=h_row[:, t, at], in0=y_acc[:, t, half, :],
                                                   scalar=RMS_ROOT * PHASES[p][2], in1=g_post[:, at],
                                                   op0=ALU.mult, op1=ALU.mult).then_inc(y_gained, 1)

            def update_x(p, t):
                dve.wait_ge(y_rs_made, 2 * p + t + 1)
                dve.wait_ge(y_gained, 4 * p + 2 * t + 2)
                for half in range(2):
                    at = slice(half * COLS, (half + 1) * COLS)
                    nc.vector.scalar_tensor_tensor(out=x_res[:, t, at], in0=h_row[:, t, at], scalar=y_rs[:, t:t + 1],
                                                   in1=x_res[:, t, at], op0=ALU.mult, op1=ALU.add).then_inc(x_updated, 1)

            def norm_x(b, t):
                dve.wait_ge(x_rs_made, 2 * b + t + 1)
                if t == 0:
                    dve.wait_ge(pre_loaded, 16 * (b + 1))
                if b > 0:
                    dve.wait_ge(x_updated, 4 * (b - 1) + 2 * t + 2)
                for half in range(2):
                    at = slice(half * COLS, (half + 1) * COLS)
                    nc.vector.scalar_tensor_tensor(out=h_row[:, t, at], in0=x_res[:, t, at], scalar=x_rs[:, t:t + 1],
                                                   in1=g_pre[:, at], op0=ALU.mult, op1=ALU.mult).then_inc(h_made, 1)

            def turned_lo(b, t):
                for half in range(2):
                    dve.wait_ge(hT_hi_made, 4 * b + 2 * t + half + 1)
                    at = (slice(None), slice(4 * half, 4 * half + 4), slice(t * P, (t + 1) * P))
                    nc.vector.scalar_tensor_tensor(out=hT_lo[at], in0=turn_banks(t, half).rearrange("p (k n) -> p k n", k=4),
                                                   scalar=RMS_ROOT, in1=hT_hi[at].bitcast(F32),
                                                   op0=ALU.mult, op1=ALU.subtract).then_inc(hT_lo_made, 1)

            def kv_rows(t):
                dve.wait_ge(h_turned, 4 * KV_PHASE + 2 * t + 2)
                if t == 0:
                    dve.wait_ge(kv_gain_loaded, 16)
                nc.vector.scalar_tensor_tensor(out=h_row[:, t, :], in0=x_res[:, t, :], scalar=x_rs[:, t:t + 1],
                                               in1=g_kv[:], op0=ALU.mult, op1=ALU.mult).then_inc(kvh_made, 1)

            def kv_lo(i):
                t, half = i // 2, i % 2
                dve.wait_ge(kvT_hi_made, i + 1)
                at = (slice(None), slice(4 * half, 4 * half + 4), slice(t * P, (t + 1) * P))
                nc.vector.scalar_tensor_tensor(out=kvT_lo[at], in0=aux[:, 1, :].rearrange("p (k n) -> p k n", k=4),
                                               scalar=RMS_ROOT, in1=kvT_hi[at].bitcast(F32),
                                               op0=ALU.mult, op1=ALU.subtract).then_inc(kvT_lo_made, 1)

            norm_x(0, 0)
            norm_x(0, 1)
            entry_lo(0, 0, 0)
            turned_lo(0, 0)
            entry_lo(0, 0, 1, empty=True)
            turned_lo(0, 1)
            for p, (kind, w, _) in enumerate(PHASES):
                t0, m0, g0, q0, n = TURN0[p], MID0[p], GATE0[p], PAIR0[p], STEPS[p]
                more = p + 1 < NP
                if kind == FFN:
                    def ffn_step(s):
                        entry_lo(p, s, 0)
                        gate(g0 + s - 1, m0 + s - 1)
                        entry_lo(p, s, 1)
                        middle_lo(m0 + s - 1, 2 * SEQ, 0)
                        exit_lo(p, s)

                    if p == KV_PHASE:
                        kv_rows(0)
                        kv_lo(0)
                        entry_lo(p, 1, 0)
                        kv_rows(1)
                        gate(g0, m0)
                        kv_lo(1)
                        entry_lo(p, 1, 1)
                        middle_lo(m0, 2 * SEQ, 0)
                        exit_lo(p, 1)
                        kv_lo(2)
                        kv_lo(3)
                    else:
                        ffn_step(1)
                    with nc.vector.Fori(2, n) as s:
                        ffn_step(s)
                    tail_lo(p)
                    gate_block(p, 0)
                    tail_middle_lo(p, 0)
                    if more:
                        entry_lo(p + 1, 0, 0)
                    gain_y(p, 0)
                    update_x(p, 0)
                    gate_block(p, 1)
                    if more:
                        norm_x(p + 1, 0)
                    tail_middle_lo(p, 1)
                    if more:
                        entry_lo(p + 1, 0, 1, empty=True)
                        turned_lo(p + 1, 0)
                    gain_y(p, 1)
                    update_x(p, 1)
                    if more:
                        norm_x(p + 1, 1)
                        turned_lo(p + 1, 1)
                else:
                    entry_lo(p, 1, 0)
                    if kind == DIFF:
                        dve.wait_ge(tables_loaded, 64)
                        for j in range(2):
                            at = 2 * j * HEAD
                            nc.vector.tensor_tensor_reduce(lam_pr[:, j * HEAD:(j + 1) * HEAD], lam_in[:, at:at + HEAD],
                                                           lam_in[:, at + HEAD:at + 2 * HEAD], 1.0, 0.0,
                                                           ALU.mult, ALU.add, lam_e[:, j:j + 1]).then_inc(lam_dot, 1)
                        nc.vector.tensor_scalar(g_sub[:], g_sub[:], (1.0 - LAM_INIT) * (2 * HEAD) ** 0.5, None, ALU.mult)\
                            .then_inc(lam_step, 1)
                        dve.wait_ge(lam_exp, 1)
                        nc.vector.tensor_tensor(neg_lam[:], lam_e[:, 1:2], lam_e[:, 0:1], ALU.subtract).then_inc(lam_step, 1)
                        dve.wait_ge(lam_step, 2)
                        nc.vector.tensor_scalar(neg_lam[:], neg_lam[:], -LAM_INIT, None, ALU.add).then_inc(lam_made, 1)
                        dve.wait_ge(lam_made, 1)
                    copy_qkv1(q0, t0 + 2)
                    entry_lo(p, 1, 1, empty=True)
                    masked_max(q0)
                    normalise(q0, kind)

                    def pair_step(s):
                        entry_lo(p, s, 0)
                        copy_qkv1(q0 + s - 1, t0 + 3 * s - 1)
                        entry_lo(p, s, 1)
                        divide_o(q0 + s - 2, kind, (m_turned, m0 + s - 2))
                        norm_o(q0 + s - 2, kind)
                        exit_lo(p, s)
                        middle_lo(m0 + s - 2, SEQ, 1)
                        masked_max(q0 + s - 1)
                        normalise(q0 + s - 1, kind)

                    with nc.vector.Fori(2, n) as s:
                        pair_step(s)
                    copy_qkv1(q0 + n - 1, t0 + 3 * n - 1)
                    tail_lo(p)
                    divide_o(q0 + n - 2, kind, (m_turned, m0 + n - 2))
                    norm_o(q0 + n - 2, kind)
                    tail_middle_lo(p, 0)
                    masked_max(q0 + n - 1)
                    normalise(q0 + n - 1, kind)
                    entry_lo(p + 1, 0, 0)
                    divide_o(q0 + n - 1, kind, (t_turned, 2 * p + 1))
                    norm_o(q0 + n - 1, kind)
                    tail_middle_lo(p, 1)
                    gain_y(p, 0)
                    gain_y(p, 1)
                    update_x(p, 0)
                    update_x(p, 1)
                    norm_x(p + 1, 0)
                    norm_x(p + 1, 1)
                    entry_lo(p + 1, 0, 1, empty=True)
                    turned_lo(p + 1, 0)
                    turned_lo(p + 1, 1)

        @block.gpsimd
        def _(pool):
            nc.gpsimd.memset(minus_half[:], -0.5).then_inc(const_step, 1)
            nc.gpsimd.memset(ident[:], 0.0).then_inc(const_step, 1)
            nc.gpsimd.memset(causal[:], 0.0).then_inc(const_step, 1)
            nc.gpsimd.memset(eps_sum[:], 2 * HEAD * EPS).then_inc(const_step, 1)
            pool.wait_ge(const_step, 4)
            nc.gpsimd.affine_select(out=ident[:], in_=ident[:], compare_op=ALU.not_equal, fill=1.0, base=0,
                                    pattern=[[-1, P]], channel_multiplier=1).then_inc(consts_made, 1)
            nc.gpsimd.affine_select(out=causal[:, P:2 * P], in_=causal[:, P:2 * P], compare_op=ALU.is_ge, fill=-FLT_MAX,
                                    base=0, pattern=[[-1, P]], channel_multiplier=1).then_inc(consts_made, 1)

            def inverse_root(dst, tmp, sums, summed, made, n):
                nc.gpsimd.tensor_scalar(tmp, sums[:, 0:1], sums[:, 1:2], D * EPS, ALU.add, ALU.add).then_inc(summed, 1)
                pool.wait_ge(summed, n)
                nc.gpsimd.tensor_tensor(dst, tmp, minus_half[:, 0:1], ALU.pow).then_inc(made, 1)

            def y_root(p, t):
                pool.wait_ge(y_squared, 4 * p + 2 * t + 2)
                inverse_root(y_rs[:, t:t + 1], rs_tmp[:, t:t + 1], y_sq[:, t, :], y_rs_sum, y_rs_made, 2 * p + t + 1)

            def x_root(b, t):
                pool.wait_ge(x_squared, 4 * b + 2 * t + 2)
                inverse_root(x_rs[:, t:t + 1], rs_tmp[:, 2 + t:3 + t], x_sq[:, t, :], x_rs_sum, x_rs_made, 2 * b + t + 1)

            def rope(q):
                pool.wait_ge(qkv0_copied, 2 * q + 1)
                pool.wait_ge(qkv1_copied, 2 * q + 1)
                if positive(q):
                    pool.wait_ge(qk_turned, q)
                src = qk_row[:].rearrange("p t (h a n) -> p t h a n", a=2, n=HALF)
                m = rope_t[:].rearrange("p t (h a n) -> p t h a n", a=2, n=HALF)
                c = cos_t[:].rearrange("p t (o n) -> p t o n", o=1).broadcast_to([P, TB, 8, HALF])
                s = sin_t[:].rearrange("p t (o n) -> p t o n", o=1).broadcast_to([P, TB, 4, HALF])
                nc.gpsimd.tensor_tensor(rope_u[:].rearrange("p t (h n) -> p t h n", n=HALF),
                                        qk_row[:].rearrange("p t (h n) -> p t h n", n=HALF), c, ALU.mult).then_inc(rope_prods, 1)
                nc.gpsimd.tensor_tensor(m[:, :, :, 0, :], src[:, :, :, 1, :], s, ALU.mult).then_inc(rope_prods, 1)
                nc.gpsimd.tensor_tensor(m[:, :, :, 1, :], src[:, :, :, 0, :], s, ALU.mult).then_inc(rope_prods, 1)
                pool.wait_ge(rope_prods, 3 * q + 3)
                u = rope_u[:].rearrange("p t (h a n) -> p (t h) a n", a=2, n=HALF)
                m = rope_t[:].rearrange("p t (h a n) -> p (t h) a n", a=2, n=HALF)
                r = qk_rot[:].rearrange("p t (h a n) -> p (t h) a n", a=2, n=HALF)
                nc.gpsimd.tensor_tensor(r[:, :, 0, :], u[:, :, 0, :], m[:, :, 0, :], ALU.subtract).then_inc(roped, 1)
                nc.gpsimd.tensor_tensor(r[:, :, 1, :], u[:, :, 1, :], m[:, :, 1, :], ALU.add).then_inc(roped, 1)

            def o_root(q):
                pool.wait_ge(o_squared, 2 * q + 2)
                nc.gpsimd.tensor_tensor(o_ms[:], o_sq[:], eps_sum[:], ALU.add).then_inc(o_ms_made, 1)
                pool.wait_ge(o_ms_made, q + 1)
                nc.gpsimd.tensor_tensor(o_rs[:], o_ms[:], minus_half[:], ALU.pow).then_inc(o_rs_made, 1)

            x_root(0, 0)
            x_root(0, 1)
            for p, (kind, _, _) in enumerate(PHASES):
                q0, n = PAIR0[p], STEPS[p]
                if kind == FFN:
                    order = [(y_root, p, 0), (x_root, p + 1, 0), (y_root, p, 1), (x_root, p + 1, 1)]
                else:
                    if kind == DIFF:
                        pool.wait_ge(tables_loaded, 64)
                    rope(q0)
                    with nc.gpsimd.Fori(1, n) as s:
                        rope(q0 + s)
                        if kind == DIFF:
                            o_root(q0 + s - 1)
                    if kind == DIFF:
                        o_root(q0 + n - 1)
                    order = [(y_root, p, 0), (y_root, p, 1), (x_root, p + 1, 0), (x_root, p + 1, 1)]
                for root, at, t in order:
                    if root is y_root or p + 1 < NP:
                        root(at, t)

        @block.tensor
        def _(pe):
            pe.wait_ge(consts_made, 2)

            def three_passes(out_ap, hi, lo, whi, wlo, start, stop, grouped=True):
                nc.tensor.matmul(out_ap, hi, whi, start=start, stop=False, skip_group_check=not grouped)
                nc.tensor.matmul(out_ap, hi, wlo, start=False, stop=False, skip_group_check=not grouped)
                return nc.tensor.matmul(out_ap, lo, whi, start=False, stop=stop, skip_group_check=not grouped)

            def entry_tile(kind, k, t):
                kk, slot, n = k % 4, k // 4, entry_width(kind)
                whi = w_hi[:, slot, kk * n:(kk + 1) * n]
                wlo = w_lo[:, slot, kk * n:(kk + 1) * n]
                tok = slice(t * P, (t + 1) * P)
                if kind == MOBA:
                    three_passes(entry[:, t, 0:P], hT_hi[:, k, tok], hT_lo[:, k, tok], whi[:, 0:P], wlo[:, 0:P],
                                 k == 0, k == KT - 1, grouped=False)
                    return three_passes(entry[:, t, P:n], kvT_hi[:, k, tok], kvT_lo[:, k, tok], whi[:, P:n], wlo[:, P:n],
                                        False, k == KT - 1, grouped=False)
                return three_passes(entry[:, t, 0:n], hT_hi[:, k, tok], hT_lo[:, k, tok], whi, wlo, k == 0, k == KT - 1)

            def exit_tile(slot, mh, ml, k, t, start, stop):
                tok = slice(t * P, (t + 1) * P)
                for c in range(2):
                    at = slice(k * D + c * COLS, k * D + (c + 1) * COLS)
                    mm = three_passes(y_acc[:, t, c, :], mh[:, k, tok], ml[:, k, tok],
                                      w_hi[:, slot, at], w_lo[:, slot, at], start, stop)
                return mm

            def turn_act(g, m, freed):
                pe.wait_ge(act_made, g + 1)
                if freed:
                    pe.wait_ge(mT_lo_made, m)
                for k in range(2):
                    for t in range(TB):
                        tr = nc.tensor.transpose(aux[:, 0, k * SEQ + t * P:k * SEQ + (t + 1) * P],
                                                 act_row[:, t, k * P:(k + 1) * P], ident[:])
                tr.then_inc(m_turned, 1)

            def turn_act_block(p, t):
                pe.wait_ge(act_made, GATE0[p] + FSTEPS + t)
                if t == 0:
                    pe.wait_ge(mT_lo_made, MID0[p + 1])
                for k in range(2):
                    tr = nc.tensor.transpose(aux[:, t, k * P:(k + 1) * P], act_row[:, t, k * P:(k + 1) * P], ident[:])
                tr.then_inc(t_turned, 1)

            def turn_qk(q):
                pe.wait_ge(roped, 2 * q + 2)
                if positive(q):
                    pe.wait_ge(pT_copied, q)
                for j in range(2):
                    for t in range(TB):
                        tr = nc.tensor.transpose(aux[:, 0, j * SEQ + t * P:j * SEQ + (t + 1) * P],
                                                 qk_rot[:, t, j * P:(j + 1) * P], ident[:])
                tr.then_inc(qk_turned, 1)

            def turn_o(q, turned):
                pe.wait_ge(o_made, 2 * (q + 1))
                for t in range(TB):
                    tr = nc.tensor.transpose(aux[:, 1, t * P:(t + 1) * P], o_row[:, t, :], ident[:])
                tr.then_inc(turned, 1)

            def scores(q, freed=None):
                pe.wait_ge(qkT_copied, q + 1)
                if freed is not None:
                    pe.wait_ge(*freed)
                for sub in range(2):
                    rows = slice(sub * HEAD, (sub + 1) * HEAD)
                    for t in range(TB):
                        at = slice(0, P) if t == 0 else slice(P, 3 * P)
                        mm = nc.tensor.matmul(aux[:, sub, at], qkT[rows, 0, t * P:(t + 1) * P],
                                              qkT[rows, 1, 0:(t + 1) * P], start=True, stop=True)
                mm.then_inc(scores_made, 1)

            def turn_p(q, kind):
                if kind == DIFF:
                    pe.wait_ge(prob_made, 2 * (q + 1))
                else:
                    pe.wait_ge(exp_made, 4 * (q + 1))
                for sub in range(1 if kind == DIFF else 2):
                    for j in range(3):
                        tr = nc.tensor.transpose(aux[:, sub, j * P:(j + 1) * P], prob[:, sub, j * P:(j + 1) * P], ident[:])
                tr.then_inc(p_turned, 1)

            def prob_v(q, kind):
                pe.wait_ge(pT_copied, q + 1)
                pe.wait_ge(qkv0_copied, 2 * q + 2)
                pe.wait_ge(qkv1_copied, 2 * q + 2)
                n = 2 * HEAD if kind == DIFF else HEAD
                for sub in range(1 if kind == DIFF else 2):
                    cols = slice(sub * HEAD, sub * HEAD + n)
                    for t in range(TB):
                        for kb in range(t + 1):
                            piece = t + kb
                            mm = nc.tensor.matmul(aux[:, 1, t * P + sub * HEAD:t * P + sub * HEAD + n],
                                                  pT[:, sub, piece * P:(piece + 1) * P], v_row[:, kb, cols],
                                                  start=(kb == 0), stop=(kb == t))
                mm.then_inc(pv_made, 1)

            def turn_rows(b, t):
                for half in range(2):
                    pe.wait_ge(h_made, 4 * b + 2 * t + half + 1)
                    for k in range(4):
                        at = (4 * half + k) * P
                        tr = nc.tensor.transpose(turn_banks(t, half)[:, k * P:(k + 1) * P], h_row[:, t, at:at + P], ident[:])
                    tr.then_inc(h_turned, 1)

            def turn_kv(i):
                t, half = i // 2, i % 2
                pe.wait_ge(kvh_made, t + 1)
                if i > 0:
                    pe.wait_ge(kvT_lo_made, i)
                for k in range(4):
                    at = (4 * half + k) * P
                    tr = nc.tensor.transpose(aux[:, 1, k * P:(k + 1) * P], h_row[:, t, at:at + P], ident[:])
                tr.then_inc(kv_turned, 1)

            turn_rows(0, 0)
            for p, (kind, w, _) in enumerate(PHASES):
                t0, m0, g0, q0, n = TURN0[p], MID0[p], GATE0[p], PAIR0[p], STEPS[p]
                more = p + 1 < NP

                def entry_step(s, between={}, empty=False):
                    for k in range(KT):
                        if k % 4 == 0:
                            pe.wait_ge(lo_made, t0 + 3 * s + k // 4 + 1)
                        for stage in between.get(k, ()):
                            stage()
                        entry_tile(kind, k, 0)
                        mm = entry_tile(kind, k, 1)
                        if k % 4 == 3:
                            mm.then_inc(w_used, 2 if empty and k == KT - 1 else 1)

                for k in range(KT):
                    if k % 4 == 0:
                        pe.wait_ge(hT_lo_made, 4 * p + k // 4 + 1)
                        pe.wait_ge(lo_made, t0 + k // 4 + 1)
                    entry_tile(kind, k, 0)
                turn_rows(p, 1)
                for k in range(KT):
                    if k % 4 == 0:
                        pe.wait_ge(hT_lo_made, 4 * p + 2 + k // 4 + 1)
                    mm = entry_tile(kind, k, 1)
                    if k % 4 == 3:
                        mm.then_inc(w_used, 1 if k < KT - 1 else 2)
                        if p == KV_PHASE:
                            turn_kv(k // 4)

                if kind == FFN:
                    turn_act(g0, m0, freed=(p > 0))

                    def ffn_step(s, first=False):
                        pe.wait_ge(act_made, g0 + s)
                        entry_step(s, {4: [lambda: turn_kv(2)]} if first and p == KV_PHASE else {})
                        if first and p == KV_PHASE:
                            turn_kv(3)
                        pe.wait_ge(lo_made, t0 + 3 * s + 3)
                        pe.wait_ge(mT_lo_made, m0 + s)
                        for k in range(2):
                            for t in range(TB):
                                mm = exit_tile(2, mT_hi, mT_lo, k, t, first and k == 0, False)
                        mm.then_inc(w_used, 1)
                        turn_act(g0 + s, m0 + s, freed=True)

                    ffn_step(1, first=True)
                    with nc.tensor.Fori(2, n - 1) as s:
                        ffn_step(s)

                    s = n - 1
                    pe.wait_ge(act_made, g0 + s)
                    for k in range(KT):
                        if k % 4 == 0:
                            pe.wait_ge(lo_made, t0 + 3 * s + k // 4 + 1)
                        mm = entry_tile(kind, k, 0)
                    mm.then_inc(entry0_done, 1)
                    pe.wait_ge(lo_made, t0 + 3 * s + 3)
                    pe.wait_ge(mT_lo_made, m0 + s)
                    for k in range(2):
                        exit_tile(2, mT_hi, mT_lo, k, 0, False, False)
                    turn_act_block(p, 0)
                    for k in range(4):
                        mm = entry_tile(kind, k, 1)
                    mm.then_inc(w_used, 1)
                    pe.wait_ge(tail_lo_made, p + 1)
                    pe.wait_ge(tT_lo_made, 2 * p + 1)
                    for k in range(2):
                        mm = exit_tile(TAIL, tT_hi, tT_lo, k, 0, False, k == 1)
                    mm.then_inc(y_done, 1)
                    for k in range(4, KT):
                        mm = entry_tile(kind, k, 1)
                    mm.then_inc(w_used, 1)
                    exit_tile(2, mT_hi, mT_lo, 0, 1, False, False)
                    turn_act_block(p, 1)
                    exit_tile(2, mT_hi, mT_lo, 1, 1, False, False).then_inc(w_used, 1)
                    pe.wait_ge(tT_lo_made, 2 * p + 2)
                    exit_tile(TAIL, tT_hi, tT_lo, 0, 1, False, False)
                    if more:
                        turn_rows(p + 1, 0)
                    exit_tile(TAIL, tT_hi, tT_lo, 1, 1, False, True).then_inc(y_done, 1)
                else:
                    def entry_free(s):
                        pe.wait_ge(qkv0_copied, 2 * (q0 + s))
                        pe.wait_ge(qkv1_copied, 2 * (q0 + s))

                    entry_free(1)
                    entry_step(1, {3: [lambda: turn_qk(q0)], 4: [lambda: scores(q0)]}, empty=True)
                    turn_p(q0, kind)
                    prob_v(q0, kind)

                    def pair_step(s, first=False):
                        entry_free(s)
                        entry_step(s, {3: [lambda: turn_o(q0 + s - 2, m_turned), lambda: turn_qk(q0 + s - 1)],
                                       4: [lambda: scores(q0 + s - 1, (mT_lo_made, m0 + s - 1))]})
                        pe.wait_ge(lo_made, t0 + 3 * s + 3)
                        exit_tile(2, mT_hi, mT_lo, 0, 0, first, False)
                        turn_p(q0 + s - 1, kind)
                        exit_tile(2, mT_hi, mT_lo, 0, 1, first, False).then_inc(w_used, 1)
                        prob_v(q0 + s - 1, kind)

                    pair_step(2, first=True)
                    with nc.tensor.Fori(3, n) as s:
                        pair_step(s)

                    turn_o(q0 + n - 2, t_turned)
                    pe.wait_ge(tail_lo_made, p + 1)
                    pe.wait_ge(tT_lo_made, 2 * p + 1)
                    exit_tile(TAIL, tT_hi, tT_lo, 0, 0, False, False)
                    turn_qk(q0 + n - 1)
                    exit_tile(TAIL, tT_hi, tT_lo, 0, 1, False, False)
                    scores(q0 + n - 1)
                    turn_p(q0 + n - 1, kind)
                    prob_v(q0 + n - 1, kind)
                    turn_o(q0 + n - 1, t_turned)
                    pe.wait_ge(tT_lo_made, 2 * p + 2)
                    for t in range(TB):
                        exit_tile(TAIL, tT_hi, tT_lo, 1, t, False, True).then_inc(y_done, 1)
                    turn_rows(p + 1, 0)


_INS = ["x", "ffn_norm", "ffn_w_in", "ffn_w_out", "mix_norm", "diff_w_qkv", "diff_lambda", "diff_subln", "diff_w_o",
        "kv_norm", "kv_w", "moba_w_q", "moba_w_o"]


def kernel(**inputs):
    import numpy as np
    import concourse.bacc as _bacc
    from concourse.bass_utils import run_bass_kernel_spmd as _run

    nc = _bacc.Bacc("TRN2", target_bir_lowering=False, num_devices=1)
    inv_freq = (1.0 / (np.float32(10000.0) ** (np.arange(0, HEAD, 2, dtype=np.float32) / np.float32(HEAD)))).astype(np.float32)
    angle = np.arange(SEQ, dtype=np.float32)[:, None] * inv_freq[None, :]
    arrays = {f"in_{n}": np.ascontiguousarray(inputs[n]) for n in _INS}
    arrays["in_rope_cos"] = np.cos(angle)
    arrays["in_rope_sin"] = np.sin(angle)
    args = [nc.dram_tensor(n, a.shape, mybir.dt.from_np(a.dtype), kind="ExternalInput").ap() for n, a in arrays.items()]
    args.append(nc.dram_tensor("out_0", (1, SEQ, D), F32, kind="ExternalOutput").ap())
    build(nc, *args)
    r = _run(nc, [arrays], core_ids=[0])
    return r.results[0]["out_0"]
```

```python
from contextlib import ExitStack

import concourse.bass as bass
from concourse import mybir

F32 = mybir.dt.float32
F32R = mybir.dt.float32r
BF16 = mybir.dt.bfloat16
ALU = mybir.AluOpType
ACT = mybir.ActivationFunctionType

P = 128
D = 1024
SEQ = 256
TB = SEQ // P
KT = D // P
HEAD = 64
HALF = HEAD // 2
PAIRS = D // (2 * HEAD)
D_FF = 2816
FC = 256
FSTEPS = D_FF // FC
COLS = 512
EPS = 1e-6
LAM_INIT = 0.2
FLT_MAX = 3.4028234663852886e38
SCALE = HEAD ** -0.5
ROOT_D = 32.0
assert ROOT_D ** 2 == D

FFN, DIFF, MOBA = "ffn", "diff", "moba"
PHASES = [(FFN, (0, 0), 0.5), (DIFF, 0, 1.0), (FFN, (0, 1), 0.5),
          (FFN, (1, 0), 0.5), (MOBA, 0, 1.0), (FFN, (1, 1), 0.5)]
NP = len(PHASES)
KV_PHASE = 3
COUNT = {FFN: FSTEPS, DIFF: PAIRS, MOBA: PAIRS + 2}
Q_STEPS = COUNT[MOBA] - PAIRS
STEPS = [COUNT[k] for k, _, _ in PHASES]


def before(per_phase):
    return [sum(per_phase(k) for k, _, _ in PHASES[:p]) for p in range(NP + 1)]


LAG = {FFN: 1, DIFF: 2, MOBA: 2 + Q_STEPS}
TURN0 = before(lambda k: 3 * COUNT[k] - LAG[k])
MID0 = before(lambda k: FSTEPS - 1 if k == FFN else PAIRS - 2)
GATE0 = before(lambda k: FSTEPS + 2 if k == FFN else 0)
PAIR0 = before(lambda k: 0 if k == FFN else PAIRS)
BLOCK0 = before(lambda k: {FFN: 2, DIFF: 1, MOBA: 3}[k])


def entry_width(kind, s):
    if kind == MOBA:
        return COLS if isinstance(s, int) and s < Q_STEPS else 2 * P
    return 2 * FC if kind == FFN else 3 * P


def fill_dmas(p, s, j):
    kind = PHASES[p][0]
    if (p, s) == (0, 0):
        return 2
    if j == 2:
        return 1
    return {FFN: 2, DIFF: 3, MOBA: 1 if s < Q_STEPS else 2}[kind]


DMAS = [fill_dmas(p, s, j) for p, (kind, _, _) in enumerate(PHASES) for s in range(STEPS[p])
        for j in range(3 if s >= LAG[kind] else 2)]


def turn_of(p, s, j):
    kind = PHASES[p][0]
    lag = LAG[kind]
    first = s if isinstance(s, int) else lag
    n = TURN0[p] + (2 * first if first < lag else 3 * first - lag) + j
    landed = 16 * sum(d for m, d in enumerate(DMAS[:n + 1]) if m % 3 == n % 3)
    if isinstance(s, int):
        return n, n % 3, landed
    return TURN0[p] - lag + j + 3 * s, n % 3, landed + 16 * DMAS[n] * (s - lag)


def positive(n):
    return not isinstance(n, int) or n > 0


def build(nc, x, ffn_norm, ffn_w_in, ffn_w_out, mix_norm, diff_w_qkv, diff_lambda, diff_subln, diff_w_o,
          kv_norm, kv_w, moba_w_q, moba_w_o, rope_cos, rope_sin, out):
    with ExitStack() as ctx:
        def sb(name, shape, dt=F32):
            return ctx.enter_context(nc.sbuf_tensor(name, shape, dt))

        def psum(name, shape):
            return ctx.enter_context(nc.psum_tensor(name, shape, F32))

        def sem(name):
            return ctx.enter_context(nc.semaphore(name))

        w_raw = sb("w_raw", [P, 4, 4 * COLS])
        w_hi = sb("w_hi", [P, 4, 4 * COLS], F32R)
        w_lo = sb("w_lo", [P, 4, 4 * COLS], F32R)
        TAIL = 3
        x_res = sb("x_res", [P, TB, D])
        h_row = sb("h_row", [P, TB, D])
        q_all = h_row
        hT_hi = sb("hT_hi", [P, KT, SEQ], F32R)
        hT_lo = sb("hT_lo", [P, KT, SEQ], F32R)
        kvT_hi = sb("kvT_hi", [P, KT, SEQ], F32R)
        kvT_lo = sb("kvT_lo", [P, KT, SEQ], F32R)
        mT_hi = sb("mT_hi", [P, 2, SEQ], F32R)
        mT_lo = sb("mT_lo", [P, 2, SEQ], F32R)
        tT_hi = sb("tT_hi", [P, 2, SEQ], F32R)
        tT_lo = sb("tT_lo", [P, 2, SEQ], F32R)
        g_post = sb("g_post", [P, D])
        g_pre = sb("g_pre", [P, D])
        g_kv = sb("g_kv", [P, D])
        g_sub = sb("g_sub", [P, P])
        sq_out_y = sb("sq_out_y", [P, TB, D], BF16)
        sq_out_x = sb("sq_out_x", [P, TB, D], BF16)
        silu_g = sb("silu_g", [P, TB, FC])
        act_row = sb("act_row", [P, TB, FC])
        qkv_row = sb("qkv_row", [P, TB, 3 * P])
        v_row = sb("v_row", [P, TB, P])
        rope_u = sb("rope_u", [P, TB, 2 * P])
        rope_t = sb("rope_t", [P, TB, 2 * P])
        qk_rot = sb("qk_rot", [P, TB, 2 * P])
        qkT = sb("qkT", [P, 2, SEQ])
        prob = sb("prob", [P, 2, 3 * P])
        pT = sb("pT", [P, 2, 3 * P])
        o_squares = sb("o_squares", [P, TB, P], BF16)
        o_row = sb("o_row", [P, TB, P])
        cos_t = sb("cos_t", [P, TB, HALF])
        sin_t = sb("sin_t", [P, TB, HALF])
        causal = sb("causal", [P, 2 * P])
        ident = sb("ident", [P, P])
        lam_in = sb("lam_in", [P, 4 * HEAD])
        lam_pr = sb("lam_pr", [P, 2 * HEAD])
        lam_e = sb("lam_e", [P, 2])
        neg_lam = sb("neg_lam", [P, 1])
        minus_half = sb("minus_half", [P, 2])
        eps_sum = sb("eps_sum", [P, 2])
        wait_pad = sb("wait_pad", [P, 2])
        y_sq = sb("y_sq", [P, TB])
        x_sq = sb("x_sq", [P, TB])
        y_rs = sb("y_rs", [P, TB])
        x_rs = sb("x_rs", [P, TB])
        kv_rs = sb("kv_rs", [P, TB])
        rs_tmp = sb("rs_tmp", [P, 2 * TB])
        row_max = sb("row_max", [P, 4])
        neg_max = sb("neg_max", [P, 4])
        row_sum = sb("row_sum", [P, 4])
        inv_sum = sb("inv_sum", [P, 4])
        mix_r = sb("mix_r", [P, 2])
        o_sq = sb("o_sq", [P, 2])
        o_ms = sb("o_ms", [P, 2])
        o_rs = sb("o_rs", [P, 2])
        o_scale = sb("o_scale", [P, 2])

        entry = psum("entry", [P, TB, COLS])
        aux = psum("aux", [P, 2, COLS])
        y_acc = psum("y_acc", [P, TB, 2, COLS])

        x_loaded = [sem("x_loaded0"), sem("x_loaded1")]
        pre_loaded = sem("pre_loaded")
        post_loaded = sem("post_loaded")
        kv_gain_loaded = sem("kv_gain_loaded")
        tables_loaded = sem("tables_loaded")
        w_loaded = [sem(f"w_loaded{i}") for i in range(3)]
        tail_loaded = sem("tail_loaded")
        stored = sem("stored")
        first_loaded = [sem("first_loaded0"), sem("first_loaded1")]
        first_hi_made = sem("first_hi_made")
        first_lo_made = sem("first_lo_made")
        hi_made = sem("hi_made")
        lo_made = sem("lo_made")
        w_used = sem("w_used")
        tail_hi_made = sem("tail_hi_made")
        tail_lo_made = sem("tail_lo_made")
        consts_made = sem("consts_made")
        const_step = sem("const_step")
        lam_dot = sem("lam_dot")
        lam_exp = sem("lam_exp")
        lam_step = sem("lam_step")
        lam_made = sem("lam_made")
        y_done = sem("y_done")
        y_squared = sem("y_squared")
        y_gained = sem("y_gained")
        eps_added = sem("eps_added")
        y_rs_made = sem("y_rs_made")
        x_updated = sem("x_updated")
        x_squared = sem("x_squared")
        x_rs_made = sem("x_rs_made")
        kv_rs_made = sem("kv_rs_made")
        h_made = sem("h_made")
        h_turned = sem("h_turned")
        hT_hi_made = sem("hT_hi_made")
        hT_lo_made = sem("hT_lo_made")
        kvh_made = sem("kvh_made")
        kv_turned = sem("kv_turned")
        kvT_hi_made = sem("kvT_hi_made")
        kvT_lo_made = sem("kvT_lo_made")
        entry0_done = sem("entry0_done")
        silu_made = sem("silu_made")
        act_made = sem("act_made")
        q0_copied = sem("q0_copied")
        q1_copied = sem("q1_copied")
        qkv0_copied = sem("qkv0_copied")
        qkv1_copied = sem("qkv1_copied")
        rope_prods = sem("rope_prods")
        roped = sem("roped")
        v_moved = sem("v_moved")
        qk_turned = sem("qk_turned")
        qkT_copied = sem("qkT_copied")
        scores_made = sem("scores_made")
        maxed = sem("maxed")
        neg_max_made = sem("neg_max_made")
        exp_made = sem("exp_made")
        inv_made = sem("inv_made")
        mix_made = sem("mix_made")
        prob_made = sem("prob_made")
        p_turned = sem("p_turned")
        pT_copied = sem("pT_copied")
        pv_made = sem("pv_made")
        o_squared = sem("o_squared")
        o_ms_made = sem("o_ms_made")
        o_rs_made = sem("o_rs_made")
        o_scale_made = sem("o_scale_made")
        o_made = sem("o_made")
        m_turned = sem("m_turned")
        mT_hi_made = sem("mT_hi_made")
        mT_lo_made = sem("mT_lo_made")
        t_turned = sem("t_turned")
        tT_hi_made = sem("tT_hi_made")
        tT_lo_made = sem("tT_lo_made")

        block = ctx.enter_context(nc.Block())

        def exit_cols(kind):
            return 2 * D if kind == FFN else D

        def tail_bank(kind, i):
            if kind == FFN:
                return aux[:, i, 0:SEQ]
            return (aux, entry)[i][:, 1, 0:SEQ]

        def turn_banks(t, half):
            return (entry, aux)[t][:, half, :]

        @block.sync
        def _(sp):
            def gain_row(p, which):
                kind, w, _ = PHASES[p]
                return ffn_norm[w[0], w[1], which:which + 1, :] if kind == FFN else \
                    mix_norm[0 if kind == DIFF else 1, which:which + 1, :]

            def load_pre(p):
                if p > 0:
                    sp.wait_ge(h_made, 4 * p)
                sp.dma_start(g_pre[:], gain_row(p, 0).broadcast_to([P, D])).then_inc(pre_loaded, 16)

            def load_post(p):
                if p > 0:
                    sp.wait_ge(y_gained, 4 * p)
                sp.dma_start(g_post[:], gain_row(p, 1).broadcast_to([P, D])).then_inc(post_loaded, 16)

            def fill(p, s, j):
                turn, slot, _ = turn_of(p, s, j)
                if not isinstance(turn, int) or turn >= 3:
                    sp.wait_ge(lo_made, turn - 2)
                kind, w, _ = PHASES[p]
                for dst, src in (exit_dmas(kind, w, slot, s - LAG[kind]) if j == 2 else entry_dmas(kind, w, slot, j, s)):
                    sp.dma_start(dst, src).then_inc(w_loaded[slot], 16)

            def entry_dmas(kind, w, slot, half, s):
                k = slice(4 * half, 4 * half + 4)
                n = entry_width(kind, s)
                dst = w_raw[:, slot, 0:4 * n].rearrange("p (k n) -> p k n", k=4)
                if kind == FFN:
                    src = ffn_w_in[w[0], w[1]].rearrange("(k p) (g n) -> p k g n", p=P, g=2)
                    return [(dst[:, :, g * FC:(g + 1) * FC], src[:, k, g, bass.ds(s * FC, FC)]) for g in range(2)]
                if kind == DIFF:
                    src = diff_w_qkv[0].rearrange("(k p) (g n) -> p k g n", p=P, g=3)
                    return [(dst[:, :, g * P:(g + 1) * P], src[:, k, g, bass.ds(s * P, P)]) for g in range(3)]
                if n == COLS:
                    src = moba_w_q[0].rearrange("(k p) n -> p k n", p=P)
                    return [(dst, src[:, k, s * COLS:(s + 1) * COLS])]
                src = kv_w.rearrange("(k p) (g n) -> p k g n", p=P, g=2)
                return [(dst[:, :, g * P:(g + 1) * P], src[:, k, g, bass.ds((s - Q_STEPS) * P, P)]) for g in range(2)]

            def fill_first(half):
                for piece in range(2):
                    for dst, src in entry_dmas(FFN, PHASES[0][1], half, half, 0):
                        k = slice(2 * piece, 2 * piece + 2)
                        sp.dma_start(dst[:, k, :], src[:, k, :]).then_inc((first_loaded, w_loaded)[piece][half], 16)

            def exit_rows(kind, w):
                return ffn_w_out[w[0], w[1]] if kind == FFN else (diff_w_o if kind == DIFF else moba_w_o)[0]

            def exit_dmas(kind, w, slot, s):
                ks = exit_cols(kind) // D
                src = exit_rows(kind, w).rearrange("(s k p) n -> p s k n", p=P, k=ks)[:, bass.ds(s, 1), :, :]
                dst = w_raw[:, slot, 0:ks * D].rearrange("p (k n) -> p k n", k=ks)
                return [(dst, src.rearrange("p s k n -> p (s k) n"))]

            sp.dma_start(x_res[:, 0, :], x[0, 0:P, :]).then_inc(x_loaded[0], 16)
            load_pre(0)
            fill_first(0)
            fill_first(1)
            sp.dma_start(x_res[:, 1, :], x[0, P:2 * P, :]).then_inc(x_loaded[1], 16)
            for p, (kind, w, _) in enumerate(PHASES):
                lag = LAG[kind]
                for s in range(1 if p == 0 else 0, lag):
                    fill(p, s, 0)
                    fill(p, s, 1)
                if p == 0:
                    fill(p, 1, 0)
                    fill(p, 1, 1)
                    fill(p, 1, 2)
                    sp.dma_start(g_kv[:], kv_norm.rearrange("(a n) -> a n", a=1).broadcast_to([P, D])).then_inc(kv_gain_loaded, 16)
                    sp.dma_start(cos_t[:], rope_cos.rearrange("(t p) n -> p t n", p=P)).then_inc(tables_loaded, 16)
                    sp.dma_start(sin_t[:], rope_sin.rearrange("(t p) n -> p t n", p=P)).then_inc(tables_loaded, 16)
                    sp.dma_start(lam_in[:], diff_lambda.rearrange("a b c -> a (b c)").broadcast_to([P, 4 * HEAD])).then_inc(tables_loaded, 16)
                    sp.dma_start(g_sub[:], diff_subln.broadcast_to([P, P])).then_inc(tables_loaded, 16)
                with nc.sync.Fori(lag + (p == 0), lag + 2) as s:
                    for j in range(3):
                        fill(p, s, j)
                load_post(p)
                if p + 1 < NP:
                    load_pre(p + 1)
                if p > 0:
                    sp.wait_ge(tail_lo_made, p)
                sp.dma_start(w_raw[:, TAIL, :].rearrange("p (k n) -> p k n", k=2),
                             exit_rows(kind, w).rearrange("(k p) n -> p k n", p=P)[:, -2:, :]).then_inc(tail_loaded, 16)
                with nc.sync.Fori(lag + 2, STEPS[p]) as s:
                    for j in range(3):
                        fill(p, s, j)
            for t in range(TB):
                for half in range(2):
                    at = slice(half * COLS, (half + 1) * COLS)
                    sp.wait_ge(x_updated, 4 * (NP - 1) + 2 * t + half + 1)
                    sp.dma_start(out[0, t * P:(t + 1) * P, at], x_res[:, t, at]).then_inc(stored, 16)
            sp.wait_ge(stored, 16 * 2 * TB)

        @block.scalar
        def _(act):
            def split_hi(p, s, j):
                kind = PHASES[p][0]
                cols = exit_cols(kind) if j == 2 else 4 * entry_width(kind, s)
                turn, slot, landed = turn_of(p, s, j)
                act.wait_ge(w_loaded[slot], landed)
                if not isinstance(turn, int) or turn >= 3:
                    act.wait_ge(w_used, turn - 2)
                    act.wait_ge(lo_made, turn - 2)
                nc.scalar.activation(w_hi[:, slot, 0:cols], w_raw[:, slot, 0:cols], ACT.Copy).then_inc(hi_made, 1)

            def first_hi(half, piece):
                act.wait_ge((first_loaded, w_loaded)[piece][half], 32)
                at = slice(piece * 2 * COLS, (piece + 1) * 2 * COLS)
                nc.scalar.activation(w_hi[:, half, at], w_raw[:, half, at], ACT.Copy)\
                    .then_inc((first_hi_made, hi_made)[piece], 1)

            def tail_hi(p):
                act.wait_ge(tail_loaded, 16 * (p + 1))
                if p > 0:
                    act.wait_ge(y_done, 2 * p)
                nc.scalar.activation(w_hi[:, TAIL, :], w_raw[:, TAIL, :], ACT.Copy).then_inc(tail_hi_made, 1)

            def silu(p, s):
                act.wait_ge(w_used, turn_of(p, s, 1)[0] + 1)
                act.wait_ge(act_made, GATE0[p] + s + 1)
                for t in range(TB):
                    ins = nc.scalar.activation(silu_g[:, t, :], entry[:, t, 0:FC], ACT.Silu, scale=x_rs[:, t:t + 1])
                ins.then_inc(silu_made, 1)

            def silu_block(p, s, t):
                g = GATE0[p] + (0 if s == 0 else FSTEPS) + t
                if t == 0:
                    act.wait_ge(entry0_done, BLOCK0[p] + (1 if s == 0 else 2))
                else:
                    act.wait_ge(w_used, turn_of(p, s, 1)[0] + 1)
                if s == 0:
                    act.wait_ge(x_rs_made, 2 * p + t + 1)
                if g >= 2:
                    act.wait_ge(act_made, g if s > 0 else g - 1)
                nc.scalar.activation(silu_g[:, t, :], entry[:, t, 0:FC], ACT.Silu, scale=x_rs[:, t:t + 1])\
                    .then_inc(silu_made, 1)

            def middle_hi(m, cols, bank, used=None):
                act.wait_ge(m_turned, m + 1)
                if used is not None:
                    act.wait_ge(w_used, used)
                nc.scalar.activation(mT_hi[:, 0:cols // SEQ, :].rearrange("p k n -> p (k n)"), aux[:, bank, 0:cols],
                                     ACT.Copy).then_inc(mT_hi_made, 1)

            def tail_piece(buf, kind, i):
                return buf[:, :, i * P:(i + 1) * P] if kind == FFN else buf[:, i:i + 1, :]

            def tail_middle_hi(p, i):
                kind = PHASES[p][0]
                act.wait_ge(t_turned, 2 * p + i + 1)
                src = tail_bank(kind, i).rearrange("p (k n) -> p k n", k=2 if kind == FFN else 1)
                nc.scalar.activation(tail_piece(tT_hi, kind, i), src, ACT.Copy).then_inc(tT_hi_made, 1)

            def copy_q0(p, s, done):
                act.wait_ge(*done)
                act.wait_ge(x_rs_made, 2 * p + 1)
                nc.scalar.activation(q_all[:, 0, s * COLS:(s + 1) * COLS], entry[:, 0, :], ACT.Copy, scale=x_rs[:, 0:1])\
                    .then_inc(q0_copied, 1)

            def copy_qkv0(p, kind, c, done):
                q = PAIR0[p] + c
                act.wait_ge(*done)
                if positive(q):
                    act.wait_ge(roped, 2 * q)
                    act.wait_ge(v_moved, q)
                if kind == MOBA:
                    if isinstance(c, int) and c == 0:
                        act.wait_ge(kv_rs_made, 1)
                        act.wait_ge(q0_copied, Q_STEPS)
                    nc.scalar.activation(qkv_row[:, 0, 0:P], q_all[:, 0, bass.ds(c * P, P)], ACT.Copy)
                    nc.scalar.activation(qkv_row[:, 0, P:3 * P], entry[:, 0, 0:2 * P], ACT.Copy, scale=kv_rs[:, 0:1])\
                        .then_inc(qkv0_copied, 1)
                else:
                    if isinstance(c, int) and c == 0:
                        act.wait_ge(x_rs_made, 2 * p + 1)
                    nc.scalar.activation(qkv_row[:, 0, :], entry[:, 0, 0:3 * P], ACT.Copy, scale=x_rs[:, 0:1])\
                        .then_inc(qkv0_copied, 1)

            def move_v(q):
                act.wait_ge(qkv1_copied, q + 1)
                act.wait_ge(qkv0_copied, q + 1)
                if positive(q):
                    act.wait_ge(pv_made, q)
                nc.scalar.activation(v_row[:], qkv_row[:, :, 2 * P:3 * P], ACT.Copy).then_inc(v_moved, 1)

            def copy_qkT(q, banks=aux):
                act.wait_ge(qk_turned, q + 1)
                nc.scalar.activation(qkT[:].rearrange("p a n -> p (a n)"), banks[:, 0, :], ACT.Copy).then_inc(qkT_copied, 1)

            def square_o(q, kind, banks=aux):
                if kind == DIFF:
                    act.wait_ge(pv_made, q + 1)
                    act.wait_ge(inv_made, q + 1)
                    for t in range(TB):
                        nc.scalar.activation(o_squares[:, t, :], banks[:, 1, t * P:(t + 1) * P], ACT.Square,
                                             scale=inv_sum[:, t:t + 1], accum_out=o_sq[:, t:t + 1]).then_inc(o_squared, 1)

            def exps(q):
                for sub in range(2):
                    act.wait_ge(neg_max_made, 2 * q + sub + 1)
                    for t in range(TB):
                        j = 2 * sub + t
                        at = prob[:, sub, 0:P] if t == 0 else prob[:, sub, P:3 * P]
                        nc.scalar.activation(at, at, ACT.Exp, bias=neg_max[:, j:j + 1], scale=SCALE,
                                             accum_out=row_sum[:, j:j + 1]).then_inc(exp_made, 1)

            def copy_pT(q, kind, banks=aux):
                act.wait_ge(p_turned, q + 1)
                n = 1 if kind == DIFF else 2
                nc.scalar.activation(pT[:, 0:n, :], banks[:, 0:n, 0:3 * P], ACT.Copy).then_inc(pT_copied, 1)

            def square_y(p, t):
                act.wait_ge(y_done, 2 * p + t + 1)
                nc.scalar.activation(sq_out_y[:, t, :], y_acc[:, t, :, :].rearrange("p c n -> p (c n)"), ACT.Square,
                                     scale=1.0 / ROOT_D, accum_out=y_sq[:, t:t + 1]).then_inc(y_squared, 1)

            def square_x(b, t):
                if b > 0:
                    act.wait_ge(x_updated, 4 * (b - 1) + 2 * t + 2)
                else:
                    act.wait_ge(x_loaded[t], 16)
                nc.scalar.activation(sq_out_x[:, t, :], x_res[:, t, :], ACT.Square, scale=1.0 / ROOT_D,
                                     accum_out=x_sq[:, t:t + 1]).then_inc(x_squared, 1)

            def turned_hi(b, t):
                for half in range(2):
                    act.wait_ge(h_turned, 4 * b + 2 * t + half + 1)
                    nc.scalar.activation(hT_hi[:, 4 * half:4 * half + 4, t * P:(t + 1) * P],
                                         turn_banks(t, half).rearrange("p (k n) -> p k n", k=4), ACT.Copy)\
                        .then_inc(hT_hi_made, 1)

            def kv_hi(i):
                t, half = i // 2, i % 2
                act.wait_ge(kv_turned, i + 1)
                nc.scalar.activation(kvT_hi[:, 4 * half:4 * half + 4, t * P:(t + 1) * P],
                                     aux[:, 1, :].rearrange("p (k n) -> p k n", k=4), ACT.Copy)\
                    .then_inc(kvT_hi_made, 1)

            first_hi(0, 0)
            turned_hi(0, 0)
            first_hi(0, 1)
            first_hi(1, 0)
            first_hi(1, 1)
            square_x(0, 0)
            turned_hi(0, 1)
            split_hi(0, 1, 0)
            square_x(0, 1)
            for p, (kind, w, _) in enumerate(PHASES):
                m0, q0, n, lead = MID0[p], PAIR0[p], STEPS[p], STEPS[p] - PAIRS
                if kind == FFN:
                    def exit_used(s):
                        return turn_of(p, s - 1, 2)[0] + 1

                    def ffn_step(s):
                        split_hi(p, s, 0)
                        silu(p, s - 1)
                        split_hi(p, s, 1)
                        middle_hi(m0 + s - 1, 2 * SEQ, 0, exit_used(s))
                        split_hi(p, s, 2)

                    silu_block(p, 0, 0)
                    if p == KV_PHASE:
                        kv_hi(0)
                    silu_block(p, 0, 1)
                    if p == KV_PHASE:
                        kv_hi(1)
                    split_hi(p, 1, 1)
                    middle_hi(m0, 2 * SEQ, 0)
                    if p == KV_PHASE:
                        kv_hi(2)
                    split_hi(p, 1, 2)
                    if p == KV_PHASE:
                        kv_hi(3)
                    split_hi(p, 2, 0)
                    silu(p, 1)
                    split_hi(p, 2, 1)
                    middle_hi(m0 + 1, 2 * SEQ, 0, exit_used(2))
                    split_hi(p, 2, 2)
                    with nc.scalar.Fori(3, n - 1) as s:
                        ffn_step(s)
                    tail_hi(p)
                    ffn_step(n - 1)
                    silu_block(p, n - 1, 0)
                    tail_middle_hi(p, 0)
                    if p + 1 < NP:
                        split_hi(p + 1, 0, 0)
                    square_y(p, 0)
                    silu_block(p, n - 1, 1)
                    tail_middle_hi(p, 1)
                    if p + 1 < NP:
                        split_hi(p + 1, 0, 1)
                        turned_hi(p + 1, 0)
                    square_y(p, 1)
                    if p + 1 < NP:
                        square_x(p + 1, 0)
                        turned_hi(p + 1, 1)
                        split_hi(p + 1, 1, 0)
                        square_x(p + 1, 1)
                else:
                    if kind == MOBA:
                        copy_q0(p, 0, (entry0_done, BLOCK0[p] + 1))
                        split_hi(p, 1, 1)
                        split_hi(p, 2, 0)
                        split_hi(p, 2, 1)
                        copy_q0(p, 1, (entry0_done, BLOCK0[p] + 2))
                        split_hi(p, 3, 0)
                        copy_qkv0(p, kind, 0, (entry0_done, BLOCK0[p] + 3))
                    else:
                        copy_qkv0(p, kind, 0, (entry0_done, BLOCK0[p] + 1))
                    split_hi(p, lead + 1, 1)
                    split_hi(p, lead + 2, 0)
                    move_v(q0)
                    if kind == DIFF:
                        act.wait_ge(lam_dot, 2)
                        nc.scalar.activation(lam_e[:], lam_e[:], ACT.Exp).then_inc(lam_exp, 1)
                    copy_qkT(q0)
                    exps(q0)
                    copy_qkv0(p, kind, 1, (w_used, turn_of(p, lead + 1, 1)[0] + 1))
                    copy_pT(q0, kind)
                    split_hi(p, lead + 2, 1)
                    square_o(q0, kind)
                    move_v(q0 + 1)
                    copy_qkT(q0 + 1)
                    split_hi(p, lead + 2, 2)
                    middle_hi(m0, SEQ, 1)
                    exps(q0 + 1)

                    def pair_step(c, tail=False):
                        split_hi(p, lead + c, 0)
                        copy_qkv0(p, kind, c - 1, (w_used, turn_of(p, lead + c - 1, 1)[0] + 1))
                        copy_pT(q0 + c - 2, kind)
                        split_hi(p, lead + c, 1)
                        square_o(q0 + c - 2, kind)
                        move_v(q0 + c - 1)
                        split_hi(p, lead + c, 2)
                        if tail:
                            tail_hi(p)
                        middle_hi(m0 + c - 2, SEQ, 1, turn_of(p, lead + c - 1, 2)[0] + 1)
                        copy_qkT(q0 + c - 1)
                        exps(q0 + c - 1)

                    with nc.scalar.Fori(3, PAIRS - 1) as c:
                        pair_step(c)
                    last = PAIRS - 1
                    pair_step(last, tail=True)
                    copy_qkv0(p, kind, last, (w_used, turn_of(p, n - 1, 1)[0] + 1))
                    copy_pT(q0 + last - 1, kind)
                    split_hi(p + 1, 0, 0)
                    copy_qkT(q0 + last, entry)
                    square_o(q0 + last - 1, kind)
                    move_v(q0 + last)
                    exps(q0 + last)
                    tail_middle_hi(p, 0)
                    copy_pT(q0 + last, kind, entry)
                    square_o(q0 + last, kind, entry)
                    split_hi(p + 1, 0, 1)
                    tail_middle_hi(p, 1)
                    square_y(p, 0)
                    square_y(p, 1)
                    turned_hi(p + 1, 0)
                    square_x(p + 1, 0)
                    turned_hi(p + 1, 1)
                    split_hi(p + 1, 1, 0)
                    square_x(p + 1, 1)

        @block.vector
        def _(dve):
            def split_lo(p, s, j):
                kind = PHASES[p][0]
                cols = exit_cols(kind) if j == 2 else 4 * entry_width(kind, s)
                turn, slot, _ = turn_of(p, s, j)
                dve.wait_ge(hi_made, turn + 1)
                nc.vector.tensor_tensor(w_lo[:, slot, 0:cols], w_raw[:, slot, 0:cols],
                                        w_hi[:, slot, 0:cols].bitcast(F32), ALU.subtract).then_inc(lo_made, 1)

            def first_lo(half, piece):
                dve.wait_ge((first_hi_made, hi_made)[piece], half + 1)
                at = slice(piece * 2 * COLS, (piece + 1) * 2 * COLS)
                nc.vector.tensor_tensor(w_lo[:, half, at], w_raw[:, half, at], w_hi[:, half, at].bitcast(F32),
                                        ALU.subtract).then_inc((first_lo_made, lo_made)[piece], 1)

            def tail_lo(p):
                dve.wait_ge(tail_hi_made, p + 1)
                nc.vector.tensor_tensor(w_lo[:, TAIL, :], w_raw[:, TAIL, :], w_hi[:, TAIL, :].bitcast(F32), ALU.subtract)\
                    .then_inc(tail_lo_made, 1)

            def gate_rows(t):
                return nc.vector.scalar_tensor_tensor(out=act_row[:, t, :], in0=entry[:, t, FC:2 * FC], scalar=x_rs[:, t:t + 1],
                                                      in1=silu_g[:, t, :], op0=ALU.mult, op1=ALU.mult)

            def gate(g, m):
                dve.wait_ge(silu_made, g + 1)
                dve.wait_ge(m_turned, m)
                for t in range(TB):
                    ins = gate_rows(t)
                ins.then_inc(act_made, 1)

            def gate_block(p, s, t):
                dve.wait_ge(silu_made, GATE0[p] + (0 if s == 0 else FSTEPS) + t + 1)
                if s > 0:
                    dve.wait_ge(m_turned, MID0[p + 1])
                elif p > 0 and PHASES[p - 1][0] == FFN:
                    dve.wait_ge(t_turned, 2 * p)
                if s == 0:
                    dve.wait_ge(x_rs_made, 2 * p + t + 1)
                gate_rows(t).then_inc(act_made, 1)

            def middle_lo(m, cols, bank):
                dve.wait_ge(mT_hi_made, m + 1)
                k = cols // SEQ
                nc.vector.tensor_tensor(mT_lo[:, 0:k, :].rearrange("p k n -> p (k n)"), aux[:, bank, 0:cols],
                                        mT_hi[:, 0:k, :].rearrange("p k n -> p (k n)").bitcast(F32), ALU.subtract)\
                    .then_inc(mT_lo_made, 1)

            def tail_piece(buf, kind, i):
                return buf[:, :, i * P:(i + 1) * P] if kind == FFN else buf[:, i:i + 1, :]

            def tail_middle_lo(p, i):
                kind = PHASES[p][0]
                dve.wait_ge(tT_hi_made, 2 * p + i + 1)
                src = tail_bank(kind, i).rearrange("p (k n) -> p k n", k=2 if kind == FFN else 1)
                nc.vector.tensor_tensor(tail_piece(tT_lo, kind, i), src, tail_piece(tT_hi, kind, i).bitcast(F32),
                                        ALU.subtract).then_inc(tT_lo_made, 1)

            def copy_q1(p, s):
                dve.wait_ge(w_used, turn_of(p, s, 1)[0] + 1)
                dve.wait_ge(x_rs_made, 2 * p + 2)
                nc.vector.tensor_scalar(q_all[:, 1, s * COLS:(s + 1) * COLS], entry[:, 1, :], x_rs[:, 1:2], None, ALU.mult)\
                    .then_inc(q1_copied, 1)

            def copy_qkv1(p, kind, c):
                q = PAIR0[p] + c
                dve.wait_ge(w_used, turn_of(p, STEPS[p] - PAIRS + c, 1)[0] + 1)
                if positive(q):
                    dve.wait_ge(roped, 2 * q)
                    dve.wait_ge(v_moved, q)
                if kind == MOBA:
                    if isinstance(c, int) and c == 0:
                        dve.wait_ge(kv_rs_made, 2)
                        dve.wait_ge(q1_copied, Q_STEPS)
                    nc.vector.tensor_copy(qkv_row[:, 1, 0:P], q_all[:, 1, bass.ds(c * P, P)])
                    nc.vector.tensor_scalar(qkv_row[:, 1, P:3 * P], entry[:, 1, 0:2 * P], kv_rs[:, 1:2], None, ALU.mult)\
                        .then_inc(qkv1_copied, 1)
                else:
                    if isinstance(c, int) and c == 0:
                        dve.wait_ge(x_rs_made, 2 * p + 2)
                    nc.vector.tensor_scalar(qkv_row[:, 1, :], entry[:, 1, 0:3 * P], x_rs[:, 1:2], None, ALU.mult)\
                        .then_inc(qkv1_copied, 1)

            def rope(q):
                dve.wait_ge(qkv0_copied, q + 1)
                dve.wait_ge(qkv1_copied, q + 1)
                if positive(q):
                    dve.wait_ge(qk_turned, q)
                x = qkv_row[:, :, 0:2 * P]
                src = x.rearrange("p t (h a n) -> p t h a n", a=2, n=HALF)
                m = rope_t[:].rearrange("p t (h a n) -> p t h a n", a=2, n=HALF)
                c = cos_t[:].rearrange("p t (o n) -> p t o n", o=1).broadcast_to([P, TB, 8, HALF])
                s = sin_t[:].rearrange("p t (o n) -> p t o n", o=1).broadcast_to([P, TB, 4, HALF])
                nc.vector.tensor_tensor(rope_u[:].rearrange("p t (h n) -> p t h n", n=HALF),
                                        x.rearrange("p t (h n) -> p t h n", n=HALF), c, ALU.mult).then_inc(rope_prods, 1)
                nc.vector.tensor_tensor(m[:, :, :, 0, :], src[:, :, :, 1, :], s, ALU.mult).then_inc(rope_prods, 1)
                nc.vector.tensor_tensor(m[:, :, :, 1, :], src[:, :, :, 0, :], s, ALU.mult).then_inc(rope_prods, 1)
                dve.wait_ge(rope_prods, 3 * q + 3)
                u = rope_u[:].rearrange("p t (h a n) -> p (t h) a n", a=2, n=HALF)
                m = rope_t[:].rearrange("p t (h a n) -> p (t h) a n", a=2, n=HALF)
                r = qk_rot[:].rearrange("p t (h a n) -> p (t h) a n", a=2, n=HALF)
                nc.vector.tensor_tensor(r[:, :, 0, :], u[:, :, 0, :], m[:, :, 0, :], ALU.subtract).then_inc(roped, 1)
                nc.vector.tensor_tensor(r[:, :, 1, :], u[:, :, 1, :], m[:, :, 1, :], ALU.add).then_inc(roped, 1)

            def masked_max(q, banks=aux):
                dve.wait_ge(scores_made, q + 1)
                if positive(q):
                    dve.wait_ge(p_turned, q)
                nc.vector.tensor_copy(wait_pad[:, 0:1], causal[:, 0:1])
                for sub in range(2):
                    for t in range(TB):
                        j = 2 * sub + t
                        at = slice(0, P) if t == 0 else slice(P, 3 * P)
                        mask = causal[:, P:2 * P] if t == 0 else causal[:, :]
                        nc.vector.tensor_tensor_reduce(prob[:, sub, at], banks[:, sub, at], mask, 1.0, -FLT_MAX,
                                                       ALU.add, ALU.max, row_max[:, j:j + 1]).then_inc(maxed, 1)
                    dve.wait_ge(maxed, 4 * q + 2 * sub + 2)
                    nc.vector.tensor_scalar(neg_max[:, 2 * sub:2 * sub + 2], row_max[:, 2 * sub:2 * sub + 2], -SCALE, None,
                                            ALU.mult).then_inc(neg_max_made, 1)

            def normalise(q, kind):
                dve.wait_ge(exp_made, 4 * q + 4)
                nc.vector.reciprocal(inv_sum[:], row_sum[:]).then_inc(inv_made, 1)
                if kind == DIFF:
                    dve.wait_ge(inv_made, q + 1)
                    nc.vector.scalar_tensor_tensor(out=mix_r[:], in0=row_sum[:, 0:2], scalar=neg_lam[:, 0:1],
                                                   in1=inv_sum[:, 2:4], op0=ALU.mult, op1=ALU.mult).then_inc(mix_made, 1)
                    dve.wait_ge(mix_made, q + 1)
                    for t, at in enumerate((slice(0, P), slice(P, 3 * P))):
                        nc.vector.scalar_tensor_tensor(out=prob[:, 0, at], in0=prob[:, 1, at], scalar=mix_r[:, t:t + 1],
                                                       in1=prob[:, 0, at], op0=ALU.mult, op1=ALU.add).then_inc(prob_made, 1)

            def norm_o(q, kind, made, banks=aux):
                o_ps = banks[:, 1, 0:2 * P]
                dve.wait_ge(*made)
                if kind == DIFF:
                    dve.wait_ge(o_rs_made, q + 1)
                    nc.vector.tensor_tensor(o_scale[:], o_rs[:], inv_sum[:, 0:2], ALU.mult).then_inc(o_scale_made, 1)
                    dve.wait_ge(o_scale_made, q + 1)
                    for t in range(TB):
                        nc.vector.scalar_tensor_tensor(out=o_row[:, t, :], in0=o_ps[:, t * P:(t + 1) * P],
                                                       scalar=o_scale[:, t:t + 1], in1=g_sub[:],
                                                       op0=ALU.mult, op1=ALU.mult).then_inc(o_made, 1)
                else:
                    dve.wait_ge(pv_made, q + 1)
                    dve.wait_ge(inv_made, q + 1)
                    for t in range(TB):
                        for sub in range(2):
                            at = slice(t * P + sub * HEAD, t * P + (sub + 1) * HEAD)
                            ins = nc.vector.tensor_scalar(o_row[:, t, sub * HEAD:(sub + 1) * HEAD], o_ps[:, at],
                                                          inv_sum[:, 2 * sub + t:2 * sub + t + 1], None, ALU.mult)
                        ins.then_inc(o_made, 1)

            def gain_y(p, t):
                dve.wait_ge(post_loaded, 16 * (p + 1))
                dve.wait_ge(y_squared, 2 * p + t + 1)
                for half in range(2):
                    at = slice(half * COLS, (half + 1) * COLS)
                    nc.vector.scalar_tensor_tensor(out=h_row[:, t, at], in0=y_acc[:, t, half, :],
                                                   scalar=PHASES[p][2], in1=g_post[:, at],
                                                   op0=ALU.mult, op1=ALU.mult).then_inc(y_gained, 1)

            def update_x(p, t, half):
                dve.wait_ge(y_rs_made, 2 * p + t + 1)
                dve.wait_ge(y_gained, 4 * p + 2 * t + half + 1)
                at = slice(half * COLS, (half + 1) * COLS)
                nc.vector.scalar_tensor_tensor(out=x_res[:, t, at], in0=h_row[:, t, at], scalar=y_rs[:, t:t + 1],
                                               in1=x_res[:, t, at], op0=ALU.mult, op1=ALU.add).then_inc(x_updated, 1)

            def gain_x(b, t, half):
                if b > 0:
                    dve.wait_ge(x_updated, 4 * (b - 1) + 2 * t + half + 1)
                else:
                    dve.wait_ge(x_loaded[t], 16)
                dve.wait_ge(pre_loaded, 16 * (b + 1))
                at = slice(half * COLS, (half + 1) * COLS)
                nc.vector.tensor_tensor(h_row[:, t, at], x_res[:, t, at], g_pre[:, at], ALU.mult).then_inc(h_made, 1)

            def update_and_gain(p, t, between=()):
                for half in range(2):
                    update_x(p, t, half)
                    if p + 1 < NP:
                        gain_x(p + 1, t, half)
                    if half == 0:
                        for stage in between:
                            stage()

            def turned_lo(b, t, halves=(0, 1)):
                for half in halves:
                    dve.wait_ge(hT_hi_made, 4 * b + 2 * t + half + 1)
                    at = (slice(None), slice(4 * half, 4 * half + 4), slice(t * P, (t + 1) * P))
                    nc.vector.tensor_tensor(hT_lo[at], turn_banks(t, half).rearrange("p (k n) -> p k n", k=4),
                                            hT_hi[at].bitcast(F32), ALU.subtract).then_inc(hT_lo_made, 1)

            def kv_rows(t):
                dve.wait_ge(h_turned, 4 * KV_PHASE + 2 * t + 2)
                if t == 0:
                    dve.wait_ge(kv_gain_loaded, 16)
                nc.vector.tensor_tensor(h_row[:, t, :], x_res[:, t, :], g_kv[:], ALU.mult).then_inc(kvh_made, 1)

            def kv_lo(i):
                t, half = i // 2, i % 2
                dve.wait_ge(kvT_hi_made, i + 1)
                at = (slice(None), slice(4 * half, 4 * half + 4), slice(t * P, (t + 1) * P))
                nc.vector.tensor_tensor(kvT_lo[at], aux[:, 1, :].rearrange("p (k n) -> p k n", k=4),
                                        kvT_hi[at].bitcast(F32), ALU.subtract).then_inc(kvT_lo_made, 1)

            gain_x(0, 0, 0)
            gain_x(0, 0, 1)
            first_lo(0, 0)
            turned_lo(0, 0)
            first_lo(0, 1)
            first_lo(1, 0)
            first_lo(1, 1)
            gain_x(0, 1, 0)
            gain_x(0, 1, 1)
            turned_lo(0, 1)
            split_lo(0, 1, 0)
            for p, (kind, w, _) in enumerate(PHASES):
                m0, g0, q0, n, lead = MID0[p], GATE0[p], PAIR0[p], STEPS[p], STEPS[p] - PAIRS
                more = p + 1 < NP
                if kind == FFN:
                    def ffn_step(s):
                        split_lo(p, s, 0)
                        gate(g0 + s, m0 + s - 1)
                        split_lo(p, s, 1)
                        middle_lo(m0 + s - 1, 2 * SEQ, 0)
                        split_lo(p, s, 2)

                    gate_block(p, 0, 0)
                    if p == KV_PHASE:
                        kv_lo(0)
                    gate_block(p, 0, 1)
                    if p == KV_PHASE:
                        kv_lo(1)
                    split_lo(p, 1, 1)
                    middle_lo(m0, 2 * SEQ, 0)
                    if p == KV_PHASE:
                        kv_lo(2)
                    split_lo(p, 1, 2)
                    if p == KV_PHASE:
                        kv_lo(3)
                    with nc.vector.Fori(2, n - 1) as s:
                        ffn_step(s)
                    tail_lo(p)
                    ffn_step(n - 1)
                    gate_block(p, n - 1, 0)
                    tail_middle_lo(p, 0)
                    if more:
                        split_lo(p + 1, 0, 0)
                    gain_y(p, 0)
                    gate_block(p, n - 1, 1)
                    update_and_gain(p, 0, between=[lambda: tail_middle_lo(p, 1)])
                    if more:
                        split_lo(p + 1, 0, 1)
                        turned_lo(p + 1, 0)
                    gain_y(p, 1)
                    if p + 1 == KV_PHASE:
                        kv_rows(0)
                    update_and_gain(p, 1)
                    if more:
                        turned_lo(p + 1, 1)
                        if p + 1 == KV_PHASE:
                            kv_rows(1)
                        split_lo(p + 1, 1, 0)
                else:
                    if kind == DIFF:
                        dve.wait_ge(tables_loaded, 64)
                        for j in range(2):
                            at = 2 * j * HEAD
                            nc.vector.tensor_tensor_reduce(lam_pr[:, j * HEAD:(j + 1) * HEAD], lam_in[:, at:at + HEAD],
                                                           lam_in[:, at + HEAD:at + 2 * HEAD], 1.0, 0.0,
                                                           ALU.mult, ALU.add, lam_e[:, j:j + 1]).then_inc(lam_dot, 1)
                        nc.vector.tensor_scalar(g_sub[:], g_sub[:], (1.0 - LAM_INIT) * (2 * HEAD) ** 0.5, None, ALU.mult)\
                            .then_inc(lam_step, 1)
                    if kind == MOBA:
                        copy_q1(p, 0)
                        split_lo(p, 1, 1)
                        split_lo(p, 2, 0)
                        split_lo(p, 2, 1)
                        copy_q1(p, 1)
                        split_lo(p, 3, 0)
                    copy_qkv1(p, kind, 0)
                    rope(q0)
                    split_lo(p, lead + 1, 1)
                    split_lo(p, lead + 2, 0)
                    if kind == DIFF:
                        dve.wait_ge(lam_exp, 1)
                        nc.vector.tensor_tensor(neg_lam[:], lam_e[:, 1:2], lam_e[:, 0:1], ALU.subtract).then_inc(lam_step, 1)
                        dve.wait_ge(lam_step, 2)
                        nc.vector.tensor_scalar(neg_lam[:], neg_lam[:], -LAM_INIT, None, ALU.add).then_inc(lam_made, 1)
                        dve.wait_ge(lam_made, 1)
                    masked_max(q0)
                    normalise(q0, kind)
                    copy_qkv1(p, kind, 1)
                    rope(q0 + 1)
                    split_lo(p, lead + 2, 1)
                    norm_o(q0, kind, (m_turned, m0))
                    middle_lo(m0, SEQ, 1)
                    split_lo(p, lead + 2, 2)
                    masked_max(q0 + 1)
                    normalise(q0 + 1, kind)

                    def pair_step(c, last=False):
                        copy_qkv1(p, kind, c - 1)
                        split_lo(p, lead + c, 0)
                        rope(q0 + c - 1)
                        norm_o(q0 + c - 2, kind, (m_turned, m0 + c - 2))
                        split_lo(p, lead + c, 1)
                        middle_lo(m0 + c - 2, SEQ, 1)
                        split_lo(p, lead + c, 2)
                        masked_max(q0 + c - 1)
                        if last:
                            copy_qkv1(p, kind, c)
                        normalise(q0 + c - 1, kind)

                    with nc.vector.Fori(3, PAIRS - 1) as c:
                        pair_step(c)
                    last = PAIRS - 1
                    pair_step(last, last=True)
                    rope(q0 + last)
                    split_lo(p + 1, 0, 0)
                    masked_max(q0 + last, entry)
                    norm_o(q0 + last - 1, kind, (m_turned, m0 + last - 1))
                    dve.wait_ge(o_made, 2 * (q0 + last))
                    normalise(q0 + last, kind)
                    tail_middle_lo(p, 0)
                    tail_lo(p)
                    norm_o(q0 + last, kind, (t_turned, 2 * p + 1), entry)
                    tail_middle_lo(p, 1)
                    split_lo(p + 1, 0, 1)
                    gain_y(p, 0)
                    update_and_gain(p, 0)
                    turned_lo(p + 1, 0, halves=(0,))
                    gain_y(p, 1)
                    turned_lo(p + 1, 0, halves=(1,))
                    update_and_gain(p, 1)
                    turned_lo(p + 1, 1)
                    split_lo(p + 1, 1, 0)

        @block.gpsimd
        def _(pool):
            nc.gpsimd.memset(minus_half[:], -0.5).then_inc(const_step, 1)
            nc.gpsimd.memset(eps_sum[:], 2 * HEAD * EPS).then_inc(const_step, 1)
            nc.gpsimd.memset(ident[:], 0.0).then_inc(const_step, 1)
            nc.gpsimd.memset(causal[:], 0.0).then_inc(const_step, 1)
            pool.wait_ge(const_step, 4)
            nc.gpsimd.affine_select(out=ident[:], in_=ident[:], compare_op=ALU.not_equal, fill=1.0, base=0,
                                    pattern=[[-1, P]], channel_multiplier=1).then_inc(consts_made, 1)
            nc.gpsimd.affine_select(out=causal[:, P:2 * P], in_=causal[:, P:2 * P], compare_op=ALU.is_ge, fill=-FLT_MAX,
                                    base=0, pattern=[[-1, P]], channel_multiplier=1).then_inc(consts_made, 1)

            def inverse_root(dst, tmp, mean_square, count):
                nc.gpsimd.tensor_scalar(tmp, mean_square, EPS, None, ALU.add).then_inc(eps_added, 1)
                pool.wait_ge(eps_added, count)
                return nc.gpsimd.tensor_tensor(dst, tmp, minus_half[:, 0:1], ALU.pow)

            def y_root(p, t):
                pool.wait_ge(y_squared, 2 * p + t + 1)
                inverse_root(y_rs[:, t:t + 1], rs_tmp[:, t:t + 1], y_sq[:, t:t + 1], 2 * (2 * p + 1) + t + 1).then_inc(y_rs_made, 1)

            def x_root(b, t):
                pool.wait_ge(x_squared, 2 * b + t + 1)
                inverse_root(x_rs[:, t:t + 1], rs_tmp[:, 2 + t:3 + t], x_sq[:, t:t + 1], 4 * b + t + 1).then_inc(x_rs_made, 1)
                if b == KV_PHASE:
                    nc.gpsimd.tensor_tensor(kv_rs[:, t:t + 1], rs_tmp[:, 2 + t:3 + t], minus_half[:, 0:1], ALU.pow)\
                        .then_inc(kv_rs_made, 1)

            def o_root(q):
                pool.wait_ge(o_squared, 2 * q + 2)
                nc.gpsimd.tensor_tensor(o_ms[:], o_sq[:], eps_sum[:], ALU.add).then_inc(o_ms_made, 1)
                pool.wait_ge(o_ms_made, q + 1)
                nc.gpsimd.tensor_tensor(o_rs[:], o_ms[:], minus_half[:], ALU.pow).then_inc(o_rs_made, 1)

            x_root(0, 0)
            x_root(0, 1)
            for p, (kind, _, _) in enumerate(PHASES):
                q0, n = PAIR0[p], PAIRS
                if kind == DIFF:
                    with nc.gpsimd.Fori(0, n) as s:
                        o_root(q0 + s)
                order = [(y_root, p, 0), (y_root, p, 1), (x_root, p + 1, 0), (x_root, p + 1, 1)]
                for root, at, t in order:
                    if root is y_root or p + 1 < NP:
                        root(at, t)

        @block.tensor
        def _(pe):
            pe.wait_ge(consts_made, 2)

            def three_passes(out_ap, hi, lo, whi, wlo, start, stop):
                nc.tensor.matmul(out_ap, hi, whi, start=start, stop=False)
                nc.tensor.matmul(out_ap, hi, wlo, start=False, stop=False)
                return nc.tensor.matmul(out_ap, lo, whi, start=False, stop=stop)

            def entry_tile(kind, s, slot, k, t):
                kk, n = k % 4, entry_width(kind, s)
                at = slice(kk * n, (kk + 1) * n)
                tok = slice(t * P, (t + 1) * P)
                hi, lo = (kvT_hi, kvT_lo) if kind == MOBA and n != COLS else (hT_hi, hT_lo)
                return three_passes(entry[:, t, 0:n], hi[:, k, tok], lo[:, k, tok], w_hi[:, slot, at], w_lo[:, slot, at],
                                    k == 0, k == KT - 1)

            def exit_tile(slot, mh, ml, k, t, start, stop):
                tok = slice(t * P, (t + 1) * P)
                at = [slice(k * D + c * COLS, k * D + (c + 1) * COLS) for c in range(2)]
                for c in range(2):
                    nc.tensor.matmul(y_acc[:, t, c, :], mh[:, k, tok], w_hi[:, slot, at[c]], start=start, stop=False)
                    nc.tensor.matmul(y_acc[:, t, c, :], mh[:, k, tok], w_lo[:, slot, at[c]], start=False, stop=False)
                for c in range(2):
                    mm = nc.tensor.matmul(y_acc[:, t, c, :], ml[:, k, tok], w_hi[:, slot, at[c]], start=False, stop=stop)
                return mm

            def turn_act(g, m):
                pe.wait_ge(act_made, g + 1)
                if positive(m):
                    pe.wait_ge(mT_lo_made, m)
                for k in range(2):
                    for t in range(TB):
                        tr = nc.tensor.transpose(aux[:, 0, k * SEQ + t * P:k * SEQ + (t + 1) * P],
                                                 act_row[:, t, k * P:(k + 1) * P], ident[:])
                tr.then_inc(m_turned, 1)

            def turn_act_block(p, t):
                pe.wait_ge(act_made, GATE0[p] + FSTEPS + t + 1)
                if t == 0:
                    pe.wait_ge(mT_lo_made, MID0[p + 1])
                for k in range(2):
                    tr = nc.tensor.transpose(aux[:, t, k * P:(k + 1) * P], act_row[:, t, k * P:(k + 1) * P], ident[:])
                tr.then_inc(t_turned, 1)

            def turn_qk(q, banks=aux):
                pe.wait_ge(roped, 2 * q + 2)
                if banks is aux and positive(q):
                    pe.wait_ge(pT_copied, q)
                for j in range(2):
                    for t in range(TB):
                        tr = nc.tensor.transpose(banks[:, 0, j * SEQ + t * P:j * SEQ + (t + 1) * P],
                                                 qk_rot[:, t, j * P:(j + 1) * P], ident[:])
                tr.then_inc(qk_turned, 1)

            def turn_o(q, turned, banks=aux):
                pe.wait_ge(o_made, 2 * (q + 1))
                for t in range(TB):
                    tr = nc.tensor.transpose(banks[:, 1, t * P:(t + 1) * P], o_row[:, t, :], ident[:])
                tr.then_inc(turned, 1)

            def scores(q, freed=None, banks=aux):
                pe.wait_ge(qkT_copied, q + 1)
                if freed is not None:
                    pe.wait_ge(*freed)
                for sub in range(2):
                    rows = slice(sub * HEAD, (sub + 1) * HEAD)
                    for t in range(TB):
                        at = slice(0, P) if t == 0 else slice(P, 3 * P)
                        mm = nc.tensor.matmul(banks[:, sub, at], qkT[rows, 0, t * P:(t + 1) * P],
                                              qkT[rows, 1, 0:(t + 1) * P], start=True, stop=True)
                mm.then_inc(scores_made, 1)

            def turn_p(q, kind, banks=aux):
                if kind == DIFF:
                    pe.wait_ge(prob_made, 2 * (q + 1))
                else:
                    pe.wait_ge(exp_made, 4 * (q + 1))
                for sub in range(1 if kind == DIFF else 2):
                    for j in range(3):
                        tr = nc.tensor.transpose(banks[:, sub, j * P:(j + 1) * P], prob[:, sub, j * P:(j + 1) * P], ident[:])
                tr.then_inc(p_turned, 1)

            def prob_v(q, kind, banks=aux):
                pe.wait_ge(pT_copied, q + 1)
                pe.wait_ge(v_moved, q + 1)
                n = 2 * HEAD if kind == DIFF else HEAD
                for sub in range(1 if kind == DIFF else 2):
                    cols = slice(sub * HEAD, sub * HEAD + n)
                    for t in range(TB):
                        for kb in range(t + 1):
                            piece = t + kb
                            mm = nc.tensor.matmul(banks[:, 1, t * P + sub * HEAD:t * P + sub * HEAD + n],
                                                  pT[:, sub, piece * P:(piece + 1) * P], v_row[:, kb, cols],
                                                  start=(kb == 0), stop=(kb == t))
                mm.then_inc(pv_made, 1)

            def turn_half(b, t, half):
                pe.wait_ge(h_made, 4 * b + 2 * t + half + 1)
                for k in range(4):
                    at = (4 * half + k) * P
                    tr = nc.tensor.transpose(turn_banks(t, half)[:, k * P:(k + 1) * P], h_row[:, t, at:at + P], ident[:])
                tr.then_inc(h_turned, 1)

            def turn_rows(b, t):
                for half in range(2):
                    turn_half(b, t, half)

            def turn_kv(i):
                t, half = i // 2, i % 2
                pe.wait_ge(kvh_made, t + 1)
                if i > 0:
                    pe.wait_ge(kvT_lo_made, i)
                else:
                    pe.wait_ge(hT_lo_made, 4 * KV_PHASE + 4)
                for k in range(4):
                    at = (4 * half + k) * P
                    tr = nc.tensor.transpose(aux[:, 1, k * P:(k + 1) * P], h_row[:, t, at:at + P], ident[:])
                tr.then_inc(kv_turned, 1)

            turn_rows(0, 0)
            for p, (kind, w, _) in enumerate(PHASES):
                m0, g0, q0, n = MID0[p], GATE0[p], PAIR0[p], STEPS[p]
                more = p + 1 < NP

                def weights_split(s, j):
                    turn, slot, _ = turn_of(p, s, j)
                    pe.wait_ge(lo_made, turn + 1)
                    return slot

                def entry_step(s, between={}, bank1_free=None, ahead=False):
                    for k in range(KT):
                        if k % 4 == 0:
                            slot = weights_split(s, k // 4)
                        if k == 2 and bank1_free is not None:
                            bank1_free()
                            entry_tile(kind, s, slot, 0, 1)
                            entry_tile(kind, s, slot, 1, 1)
                        for stage in between.get(k, ()):
                            stage()
                        mm = entry_tile(kind, s, slot, k, 0)
                        if not (k < 2 and bank1_free is not None or k >= KT - 2 and ahead):
                            mm = entry_tile(kind, s, slot, k, 1)
                        if k == 3:
                            mm.then_inc(w_used, 1)
                    if ahead:
                        mm.then_inc(entry0_done, 1)
                        for k in range(KT - 2, KT):
                            mm = entry_tile(kind, s, slot, k, 1)
                    mm.then_inc(w_used, 1)

                for k in range(KT):
                    if k % 4 == 0:
                        pe.wait_ge(hT_lo_made, 4 * p + k // 4 + 1)
                        if p > 0:
                            weights_split(0, k // 4)
                        else:
                            pe.wait_ge(first_lo_made, k // 4 + 1)
                    elif k % 4 == 2 and p == 0:
                        pe.wait_ge(lo_made, k // 4 + 1)
                    if k == KT - 1:
                        turn_half(p, 1, 0)
                    mm = entry_tile(kind, 0, turn_of(p, 0, k // 4)[1], k, 0)
                mm.then_inc(entry0_done, 1)
                turn_half(p, 1, 1)
                for k in range(KT):
                    if k % 4 == 0:
                        pe.wait_ge(hT_lo_made, 4 * p + 2 + k // 4 + 1)
                    mm = entry_tile(kind, 0, turn_of(p, 0, k // 4)[1], k, 1)
                    if k % 4 == 3:
                        mm.then_inc(w_used, 1)
                        if p == KV_PHASE:
                            turn_kv(k // 4)

                if kind == FFN:
                    def exit_step(s, first=False):
                        slot = weights_split(s, 2)
                        pe.wait_ge(mT_lo_made, m0 + s)
                        for k in range(2):
                            for t in range(TB):
                                mm = exit_tile(slot, mT_hi, mT_lo, k, t, first and k == 0, False)
                        mm.then_inc(w_used, 1)

                    def ffn_step(s):
                        pe.wait_ge(act_made, g0 + s + 1)
                        entry_step(s)
                        exit_step(s)
                        turn_act(g0 + s + 1, m0 + s)

                    pe.wait_ge(act_made, g0 + 1)
                    if p == KV_PHASE:
                        stages = {3: [lambda: turn_act(g0 + 1, m0)], 4: [lambda: turn_kv(2)], 6: [lambda: turn_kv(3)]}
                    else:
                        stages = {3: [lambda: turn_act(g0 + 1, m0)]}
                    entry_step(1, stages, bank1_free=lambda: pe.wait_ge(act_made, g0 + 2))
                    exit_step(1, first=True)
                    turn_act(g0 + 2, m0 + 1)
                    with nc.tensor.Fori(2, n - 1) as s:
                        ffn_step(s)

                    s = n - 1
                    pe.wait_ge(act_made, g0 + s + 1)
                    for k in range(KT):
                        if k % 4 == 0:
                            slot = weights_split(s, k // 4)
                        mm = entry_tile(kind, s, slot, k, 0)
                    mm.then_inc(entry0_done, 1)
                    out_slot = weights_split(s, 2)
                    pe.wait_ge(mT_lo_made, m0 + s)
                    for k in range(2):
                        exit_tile(out_slot, mT_hi, mT_lo, k, 0, False, False)
                    turn_act_block(p, 0)
                    for k in range(4):
                        mm = entry_tile(kind, s, turn_of(p, s, 0)[1], k, 1)
                    mm.then_inc(w_used, 1)
                    pe.wait_ge(tail_lo_made, p + 1)
                    pe.wait_ge(tT_lo_made, 2 * p + 1)
                    for k in range(2):
                        mm = exit_tile(TAIL, tT_hi, tT_lo, k, 0, False, k == 1)
                    mm.then_inc(y_done, 1)
                    for k in range(4, KT):
                        mm = entry_tile(kind, s, turn_of(p, s, 1)[1], k, 1)
                    mm.then_inc(w_used, 1)
                    exit_tile(out_slot, mT_hi, mT_lo, 0, 1, False, False)
                    turn_act_block(p, 1)
                    exit_tile(out_slot, mT_hi, mT_lo, 1, 1, False, False).then_inc(w_used, 1)
                    pe.wait_ge(tT_lo_made, 2 * p + 2)
                    exit_tile(TAIL, tT_hi, tT_lo, 0, 1, False, False)
                    if more:
                        turn_rows(p + 1, 0)
                    exit_tile(TAIL, tT_hi, tT_lo, 1, 1, False, True).then_inc(y_done, 1)
                else:
                    lead = n - PAIRS

                    def entry_free(c):
                        pe.wait_ge(qkv0_copied, q0 + c)
                        pe.wait_ge(qkv1_copied, q0 + c)

                    if kind == MOBA:
                        pe.wait_ge(q0_copied, 1)
                        entry_step(1, bank1_free=lambda: pe.wait_ge(q1_copied, 1), ahead=True)
                        pe.wait_ge(q0_copied, 2)
                        entry_step(2, bank1_free=lambda: pe.wait_ge(q1_copied, 2), ahead=True)

                    pe.wait_ge(qkv0_copied, q0 + 1)
                    at_scores = 5 if kind == MOBA else 4
                    entry_step(lead + 1, {3: [lambda: turn_qk(q0)], at_scores: [lambda: scores(q0)]},
                               bank1_free=lambda: pe.wait_ge(qkv1_copied, q0 + 1))
                    turn_p(q0, kind)

                    entry_free(2)
                    entry_step(lead + 2, {1: [lambda: prob_v(q0, kind)], 3: [lambda: turn_qk(q0 + 1)],
                                          4: [lambda: turn_o(q0, m_turned)],
                                          at_scores + 1: [lambda: scores(q0 + 1, (mT_lo_made, m0 + 1))]})
                    slot = weights_split(lead + 2, 2)
                    exit_tile(slot, mT_hi, mT_lo, 0, 0, True, False)
                    turn_p(q0 + 1, kind)
                    exit_tile(slot, mT_hi, mT_lo, 0, 1, True, False).then_inc(w_used, 1)
                    prob_v(q0 + 1, kind)

                    def pair_entry(c):
                        entry_free(c)
                        entry_step(lead + c, {3: [lambda: turn_o(q0 + c - 2, m_turned), lambda: turn_qk(q0 + c - 1)],
                                              5: [lambda: scores(q0 + c - 1, (mT_lo_made, m0 + c - 1))]})

                    with nc.tensor.Fori(3, PAIRS - 1) as c:
                        pair_entry(c)
                        slot = weights_split(lead + c, 2)
                        exit_tile(slot, mT_hi, mT_lo, 0, 0, False, False)
                        turn_p(q0 + c - 1, kind)
                        exit_tile(slot, mT_hi, mT_lo, 0, 1, False, False).then_inc(w_used, 1)
                        prob_v(q0 + c - 1, kind)

                    last = PAIRS - 1
                    pair_entry(last)
                    slot = weights_split(n - 1, 2)
                    exit_tile(slot, mT_hi, mT_lo, 0, 0, False, False)
                    turn_p(q0 + last - 1, kind)
                    exit_tile(slot, mT_hi, mT_lo, 0, 1, False, False).then_inc(w_used, 1)
                    entry_free(PAIRS)
                    turn_qk(q0 + last, entry)
                    prob_v(q0 + last - 1, kind)
                    scores(q0 + last, banks=entry)
                    turn_o(q0 + last - 1, t_turned)
                    turn_p(q0 + last, kind, entry)
                    prob_v(q0 + last, kind, entry)
                    pe.wait_ge(tail_lo_made, p + 1)
                    pe.wait_ge(tT_lo_made, 2 * p + 1)
                    exit_tile(TAIL, tT_hi, tT_lo, 0, 0, False, False)
                    turn_o(q0 + last, t_turned, entry)
                    pe.wait_ge(tT_lo_made, 2 * p + 2)
                    exit_tile(TAIL, tT_hi, tT_lo, 1, 0, False, True).then_inc(y_done, 1)
                    exit_tile(TAIL, tT_hi, tT_lo, 0, 1, False, False)
                    exit_tile(TAIL, tT_hi, tT_lo, 1, 1, False, True).then_inc(y_done, 1)
                    turn_rows(p + 1, 0)


_INS = ["x", "ffn_norm", "ffn_w_in", "ffn_w_out", "mix_norm", "diff_w_qkv", "diff_lambda", "diff_subln", "diff_w_o",
        "kv_norm", "kv_w", "moba_w_q", "moba_w_o"]


def kernel(**inputs):
    import numpy as np
    import concourse.bacc as _bacc
    from concourse.bass_utils import run_bass_kernel_spmd as _run

    nc = _bacc.Bacc("TRN2", target_bir_lowering=False, num_devices=1)
    inv_freq = (1.0 / (np.float32(10000.0) ** (np.arange(0, HEAD, 2, dtype=np.float32) / np.float32(HEAD)))).astype(np.float32)
    angle = np.arange(SEQ, dtype=np.float32)[:, None] * inv_freq[None, :]
    arrays = {f"in_{n}": np.ascontiguousarray(inputs[n]) for n in _INS}
    arrays["in_rope_cos"] = np.cos(angle)
    arrays["in_rope_sin"] = np.sin(angle)
    args = [nc.dram_tensor(n, a.shape, mybir.dt.from_np(a.dtype), kind="ExternalInput").ap() for n, a in arrays.items()]
    args.append(nc.dram_tensor("out_0", (1, SEQ, D), F32, kind="ExternalOutput").ap())
    build(nc, *args)
    r = _run(nc, [arrays], core_ids=[0])
    return r.results[0]["out_0"]
```
